# Optimizing a Trainium2 kernel written in Bass

```python
import jax
import jax.numpy as jnp
from jax import lax
import numpy as np

D_MODEL = 1024
BATCH = 1
SEQ = 256
DEPTH = 2

GRID_W = 64
CTX_LEN = 256
HEAD_DIM = 64
ROPE_THETA = 10000.0
EPS = 1e-6
NEG = -1e30
N_MOD = 6

A_HEADS = 8
A_KV_HEADS = 2
A_BLOCK = 128
A_WINDOW = 128
B_HEADS = 8
NA_ROWS = 8
NA_COLS = 16
C_HEADS = 4
C_DK = 128
C_DV = 256
C_GATE_RANK = 16
C_GATE_TAU = 16.0
C_CHUNK = 64
PEER_HEADS = 8
PEER_NKEYS = 128
PEER_EXPERTS = PEER_NKEYS * PEER_NKEYS
PEER_QDIM = 256
PEER_HALF = PEER_QDIM // 2
PEER_TOPK = 16
PEER_BLOCK = 128

A_Q = A_HEADS * HEAD_DIM
A_KV = A_KV_HEADS * HEAD_DIM
B_W = B_HEADS * HEAD_DIM
C_K = C_HEADS * C_DK
C_V = C_HEADS * C_DV
KV_SPLITS = (A_KV, A_KV, B_W, B_W, C_K, C_V, 2 * C_GATE_RANK)
Q_SPLITS = (A_Q, B_W, C_K, C_V, 3 * D_MODEL)
N_KV_COLS = sum(KV_SPLITS)
IN_WIDTH = N_KV_COLS + sum(Q_SPLITS)

kernel_name = 'hybrid_dit_parallel_mixers_peer'

def _rmsnorm(x, g):
    xf = x.astype(jnp.float32)
    y = xf * lax.rsqrt(jnp.mean(xf * xf, axis=-1, keepdims=True) + EPS)
    return (y * g.astype(jnp.float32)).astype(x.dtype)

def _modulate(x, g, shift, scale):
    return _rmsnorm(x, g) * (1.0 + scale) + shift

def _split(t, sizes):
    return jnp.split(t, np.cumsum(sizes)[:-1].tolist(), axis=-1)

def _heads(t, n):
    return t.reshape(t.shape[:-1] + (n, t.shape[-1] // n))

def _axial_rope(S):
    t = jnp.arange(S)
    row = (t // GRID_W).astype(jnp.float32)[:, None]
    col = (t % GRID_W).astype(jnp.float32)[:, None]
    nf = HEAD_DIM // 4
    inv = ROPE_THETA ** (-jnp.arange(nf, dtype=jnp.float32) / nf)
    ang = jnp.concatenate([row * inv, row * inv, col * inv, col * inv], axis=-1)
    return jnp.cos(ang), jnp.sin(ang)

def _rope(x, cos, sin):
    x1, x2, x3, x4 = jnp.split(x, 4, axis=-1)
    rot = jnp.concatenate([-x2, x1, -x4, x3], axis=-1)
    return (x * cos[:, None] + rot * sin[:, None]).astype(x.dtype)

def _dense_attention(q, k, v, sink):
    B, L, H, dh = q.shape
    G = k.shape[2]
    R = H // G
    s = jnp.einsum('bqgrd,bkgd->bgrqk', q.reshape(B, L, G, R, dh), k).astype(jnp.float32) * dh ** -0.5
    if sink is not None:
        s_sink = jnp.broadcast_to(sink.reshape(G, R, 1, 1).astype(jnp.float32), s.shape[:-1] + (1,))
        s = jnp.concatenate([s, s_sink], axis=-1)
    p = jax.nn.softmax(s, axis=-1)[..., :L].astype(v.dtype)
    return jnp.einsum('bgrqk,bkgd->bqgrd', p, v).reshape(B, L, H * dh)

def _window_attention(q, k, v, kc, vc, sink):
    B, S, H, dh = q.shape
    G = k.shape[2]
    R = H // G
    L = kc.shape[1]
    nb = S // A_BLOCK
    qb = q.reshape(B, nb, A_BLOCK, G, R, dh)
    pad = ((0, 0), (A_BLOCK, A_BLOCK), (0, 0), (0, 0))

    def band(t):
        tb = jnp.pad(t, pad).reshape(B, nb + 2, A_BLOCK, G, dh)
        return jnp.concatenate([tb[:, :-2], tb[:, 1:-1], tb[:, 2:]], axis=2)

    kw, vw = band(k), band(v)
    qi = jnp.arange(nb)[:, None, None] * A_BLOCK + jnp.arange(A_BLOCK)[None, :, None]
    kj = (jnp.arange(nb)[:, None, None] - 1) * A_BLOCK + jnp.arange(3 * A_BLOCK)[None, None, :]
    valid = (jnp.abs(kj - qi) <= A_WINDOW) & (kj >= 0) & (kj < S)
    scale = dh ** -0.5
    s_loc = jnp.einsum('bnqgrd,bnkgd->bngrqk', qb, kw).astype(jnp.float32) * scale
    s_loc = jnp.where(valid[None, :, None, None], s_loc, NEG)
    s_ctx = jnp.einsum('bnqgrd,bcgd->bngrqc', qb, kc).astype(jnp.float32) * scale
    s_sink = jnp.broadcast_to(sink.reshape(G, R, 1, 1).astype(jnp.float32), s_loc.shape[:-1] + (1,))
    p = jax.nn.softmax(jnp.concatenate([s_loc, s_ctx, s_sink], axis=-1), axis=-1).astype(v.dtype)
    nk = 3 * A_BLOCK
    o = (jnp.einsum('bngrqk,bnkgd->bnqgrd', p[..., :nk], vw)
         + jnp.einsum('bngrqc,bcgd->bnqgrd', p[..., nk:nk + L], vc))
    return o.reshape(B, S, H * dh)

def _neighbourhood_attention(q, k, v, kc, vc, rpb):
    B, S, H, dh = q.shape
    rows = S // GRID_W
    kh = min(NA_ROWS, rows)
    r = jnp.arange(rows)
    row_idx = jnp.clip(r - kh // 2, 0, rows - kh)[:, None] + jnp.arange(kh)[None, :]
    c = jnp.arange(GRID_W)
    col_start = jnp.clip(c - NA_COLS // 2, 0, GRID_W - NA_COLS)
    col_valid = (c[None, :] >= col_start[:, None]) & (c[None, :] < col_start[:, None] + NA_COLS)
    qg = q.reshape(B, rows, GRID_W, H, dh)
    kg = k.reshape(B, rows, GRID_W, H, dh)[:, row_idx]
    vg = v.reshape(B, rows, GRID_W, H, dh)[:, row_idx]
    scale = dh ** -0.5
    s = jnp.einsum('brqhd,brjkhd->bhrqjk', qg, kg).astype(jnp.float32) * scale
    dr = row_idx - r[:, None] + (NA_ROWS - 1)
    dc = jnp.clip(c[None, :] - c[:, None], -(NA_COLS - 1), NA_COLS - 1) + (NA_COLS - 1)
    bias = rpb[:, dr[:, None, :, None], dc[None, :, None, :]]
    s = jnp.where(col_valid[:, None, :], s + bias[None].astype(jnp.float32), NEG)
    s = s.reshape(B, H, rows, GRID_W, kh * GRID_W)
    s_ctx = jnp.einsum('brqhd,bchd->bhrqc', qg, kc).astype(jnp.float32) * scale
    p = jax.nn.softmax(jnp.concatenate([s, s_ctx], axis=-1), axis=-1).astype(v.dtype)
    nk = kh * GRID_W
    p_loc = p[..., :nk].reshape(B, H, rows, GRID_W, kh, GRID_W)
    o = (jnp.einsum('bhrqjk,brjkhd->brqhd', p_loc, vg)
         + jnp.einsum('bhrqc,bchd->brqhd', p[..., nk:], vc))
    return o.reshape(B, S, H * dh)

def _gla_decay(a, w2, b):
    z = (a @ w2 + b).astype(jnp.float32)
    return _heads(jax.nn.log_sigmoid(z) / C_GATE_TAU, C_HEADS)

def _gla_scan(q, k, v, la, s0):
    q, k, v = q.astype(jnp.float32), k.astype(jnp.float32), v.astype(jnp.float32)
    B, T, H, dk = q.shape
    dv = v.shape[-1]
    n = T // C_CHUNK

    def chunks(t):
        return t.reshape(B, n, C_CHUNK, H, t.shape[-1]).transpose(1, 0, 3, 2, 4)

    causal = jnp.tril(jnp.ones((C_CHUNK, C_CHUNK), bool))[:, :, None]

    def step(s, inp):
        qc, kc, vc, lac = inp
        b = jnp.cumsum(lac, axis=2)
        diff = jnp.where(causal, b[:, :, :, None, :] - b[:, :, None, :, :], 0.0)
        decay = jnp.where(causal, jnp.exp(diff), 0.0)
        att = jnp.einsum('bhid,bhjd,bhijd->bhij', qc, kc, decay)
        o = jnp.einsum('bhij,bhjv->bhiv', att, vc) + jnp.einsum('bhid,bhdv->bhiv', qc * jnp.exp(b), s)
        b_last = b[:, :, -1:]
        s_new = (jnp.exp(b_last[:, :, 0])[..., None] * s
                 + jnp.einsum('bhjd,bhjv->bhdv', kc * jnp.exp(b_last - b), vc))
        return s_new, o

    s_fin, o = lax.scan(step, s0, (chunks(q), chunks(k), chunks(v), chunks(la)))
    return o.transpose(1, 0, 3, 2, 4).reshape(B, T, H, dv), s_fin

def _gla_final_state(k, v, la):
    b = jnp.cumsum(la, axis=1)
    return jnp.einsum('bthd,bthv->bhdv', k.astype(jnp.float32) * jnp.exp(b[:, -1:] - b), v.astype(jnp.float32))

def _gla_out(o, r, g):
    y = _rmsnorm(o, g).astype(r.dtype) * jax.nn.silu(_heads(r, C_HEADS))
    return y.reshape(y.shape[:-2] + (C_V,))

def _flip(t):
    return jnp.flip(t, axis=1)

def _merge(oA, oB, oC, gates, p):
    gA, gB, gC = jnp.split(gates, 3, axis=-1)
    y = (jax.nn.sigmoid(gA) * (oA @ p['w_oa'])
         + jax.nn.sigmoid(gB) * (oB @ p['w_ob'])
         + jax.nn.sigmoid(gC) * (oC @ p['w_oc']))
    return y @ p['w_out']

def _token_mixers(h, hc, p, cos, sin, last):
    B = h.shape[0]
    w_in = p['w_in']
    proj = h @ w_in
    kA, vA, kB, vB, kC, vC, aC = _split(proj[..., :N_KV_COLS], KV_SPLITS)
    qA, qB, qC, rC, gates = _split(proj[..., N_KV_COLS:], Q_SPLITS)
    cproj = hc @ (w_in[:, :N_KV_COLS] if last else w_in)
    ckA, cvA, ckB, cvB, ckC, cvC, caC = _split(cproj[..., :N_KV_COLS], KV_SPLITS)
    if not last:
        cqA, cqB, cqC, crC, cgates = _split(cproj[..., N_KV_COLS:], Q_SPLITS)

    qa = _rope(_rmsnorm(_heads(qA, A_HEADS), p['qn_a']), cos, sin)
    ka = _rope(_rmsnorm(_heads(kA, A_KV_HEADS), p['kn_a']), cos, sin)
    cka = _rmsnorm(_heads(ckA, A_KV_HEADS), p['kn_a'])
    cva = _heads(cvA, A_KV_HEADS)
    oA = _window_attention(qa, ka, _heads(vA, A_KV_HEADS), cka, cva, p['sink_a'])

    qb = _rmsnorm(_heads(qB, B_HEADS), p['qn_b'])
    kb = _rmsnorm(_heads(kB, B_HEADS), p['kn_b'])
    ckb = _rmsnorm(_heads(ckB, B_HEADS), p['kn_b'])
    cvb = _heads(cvB, B_HEADS)
    oB = _neighbourhood_attention(qb, kb, _heads(vB, B_HEADS), ckb, cvb, p['rpb_b'])

    ckc, cvc = _heads(ckC, C_HEADS), _heads(cvC, C_HEADS)
    caf, cab = jnp.split(caC, 2, axis=-1)
    cla_f = _gla_decay(caf, p['wa2_f'], p['ba_f'])
    cla_b = _gla_decay(cab, p['wa2_b'], p['ba_b'])
    if last:
        s_f = _gla_final_state(ckc, cvc, cla_f)
        s_b = _gla_final_state(_flip(ckc), _flip(cvc), _flip(cla_b))
    else:
        cqc = _heads(cqC, C_HEADS) * C_DK ** -0.5
        zeros = jnp.zeros((B, C_HEADS, C_DK, C_DV), jnp.float32)
        co_f, s_f = _gla_scan(cqc, ckc, cvc, cla_f, zeros)
        co_b, s_b = _gla_scan(_flip(cqc), _flip(ckc), _flip(cvc), _flip(cla_b), zeros)
        coC = _gla_out(co_f + _flip(co_b), crC, p['gn_c'])
    qc_ = _heads(qC, C_HEADS) * C_DK ** -0.5
    kc_, vc_ = _heads(kC, C_HEADS), _heads(vC, C_HEADS)
    af, ab = jnp.split(aC, 2, axis=-1)
    la_f = _gla_decay(af, p['wa2_f'], p['ba_f'])
    la_b = _gla_decay(ab, p['wa2_b'], p['ba_b'])
    o_f, _ = _gla_scan(qc_, kc_, vc_, la_f, s_f)
    o_b, _ = _gla_scan(_flip(qc_), _flip(kc_), _flip(vc_), _flip(la_b), s_b)
    oC = _gla_out(o_f + _flip(o_b), rC, p['gn_c'])

    y = _merge(oA, oB, oC, gates, p)
    if last:
        return y, None
    coA = _dense_attention(_rmsnorm(_heads(cqA, A_HEADS), p['qn_a']), cka, cva, p['sink_a'])
    coB = _dense_attention(_rmsnorm(_heads(cqB, B_HEADS), p['qn_b']), ckb, cvb, None)
    yc = _merge(coA, coB, coC, cgates, p)
    return y, yc

def _peer(h, p):
    T, D = h.shape
    u_tab, v_tab = p['peer_u'], p['peer_v']

    def block(xb):
        q = _rmsnorm((xb @ p['w_pq']).reshape(PEER_BLOCK, PEER_HEADS, 2, PEER_HALF), p['pq_g'])
        s = jnp.einsum('tphd,phnd->tphn', q, p['sub_keys']).astype(jnp.float32)
        s1, i1 = lax.top_k(s[:, :, 0], PEER_TOPK)
        s2, i2 = lax.top_k(s[:, :, 1], PEER_TOPK)
        cand = (s1[..., :, None] + s2[..., None, :]).reshape(PEER_BLOCK, PEER_HEADS, PEER_TOPK * PEER_TOPK)
        cidx = (i1[..., :, None] * PEER_NKEYS + i2[..., None, :]).reshape(PEER_BLOCK, PEER_HEADS, PEER_TOPK * PEER_TOPK)
        top, pos = lax.top_k(cand, PEER_TOPK)
        idx = jnp.take_along_axis(cidx, pos, axis=-1)
        g = jax.nn.softmax(top, axis=-1).astype(xb.dtype)
        u = u_tab[idx]
        v = v_tab[idx]
        act = jax.nn.gelu(jnp.einsum('td,tpkd->tpk', xb, u), approximate=False)
        return jnp.einsum('tpk,tpkd->td', g * act, v)

    return lax.map(block, h.reshape(T // PEER_BLOCK, PEER_BLOCK, D)).reshape(T, D)

def _layer(x, ctx, c_act, cctx_act, p, cos, sin, last):
    B, S, D = x.shape
    L = ctx.shape[1]
    sh1, sc1, g1, sh2, sc2, g2 = jnp.split((c_act @ p['w_mod'] + p['b_mod'])[:, None, :], N_MOD, axis=-1)
    csh1, csc1, cg1, csh2, csc2, cg2 = jnp.split(cctx_act @ p['w_mod'] + p['b_mod'], N_MOD, axis=-1)
    h = _modulate(x, p['norm1'], sh1, sc1)
    hc = _modulate(ctx, p['norm1'], csh1, csc1)
    y, yc = _token_mixers(h, hc, p, cos, sin, last)
    x = x + g1 * y
    h2 = _modulate(x, p['norm2'], sh2, sc2)
    if last:
        return x + g2 * _peer(h2.reshape(B * S, D), p).reshape(B, S, D), ctx
    ctx = ctx + cg1 * yc
    hc2 = _modulate(ctx, p['norm2'], csh2, csc2)
    out = _peer(jnp.concatenate([h2.reshape(B * S, D), hc2.reshape(B * L, D)], axis=0), p)
    x = x + g2 * out[:B * S].reshape(B, S, D)
    ctx = ctx + cg2 * out[B * S:].reshape(B, L, D)
    return x, ctx

def setup_inputs(seed: int = 0) -> dict:
    key = jax.random.key(seed)
    ks = iter(jax.random.split(key, 40))

    def nrm(shape, scale):
        return jax.random.normal(next(ks), shape, jnp.float32) * scale

    D, Ly = D_MODEL, DEPTH
    return {
        'x': nrm((BATCH, SEQ, D), 1.0),
        'c': nrm((BATCH, D), 1.0),
        'ctx': nrm((BATCH, CTX_LEN, D), 1.0),
        'c_ctx': nrm((D,), 1.0),
        'w_mod': nrm((Ly, D, N_MOD * D), 0.5 * D ** -0.5),
        'b_mod': nrm((Ly, N_MOD * D), 0.02),
        'norm1': 1.0 + nrm((Ly, D), 0.05),
        'norm2': 1.0 + nrm((Ly, D), 0.05),
        'w_in': nrm((Ly, D, IN_WIDTH), D ** -0.5),
        'qn_a': 1.0 + nrm((Ly, HEAD_DIM), 0.05),
        'kn_a': 1.0 + nrm((Ly, HEAD_DIM), 0.05),
        'sink_a': nrm((Ly, A_HEADS), 0.5),
        'qn_b': 1.0 + nrm((Ly, HEAD_DIM), 0.05),
        'kn_b': 1.0 + nrm((Ly, HEAD_DIM), 0.05),
        'rpb_b': nrm((Ly, B_HEADS, 2 * NA_ROWS - 1, 2 * NA_COLS - 1), 0.1),
        'wa2_f': nrm((Ly, C_GATE_RANK, C_K), C_GATE_RANK ** -0.5),
        'ba_f': nrm((Ly, C_K), 0.1),
        'wa2_b': nrm((Ly, C_GATE_RANK, C_K), C_GATE_RANK ** -0.5),
        'ba_b': nrm((Ly, C_K), 0.1),
        'gn_c': 1.0 + nrm((Ly, C_DV), 0.05),
        'w_oa': nrm((Ly, A_Q, D), A_Q ** -0.5),
        'w_ob': nrm((Ly, B_W, D), B_W ** -0.5),
        'w_oc': nrm((Ly, C_V, D), C_V ** -0.5),
        'w_out': nrm((Ly, D, D), D ** -0.5),
        'w_pq': nrm((Ly, D, PEER_HEADS * PEER_QDIM), D ** -0.5),
        'pq_g': 1.0 + nrm((Ly, PEER_HALF), 0.05),
        'sub_keys': nrm((Ly, PEER_HEADS, 2, PEER_NKEYS, PEER_HALF), PEER_HALF ** -0.5),
        'peer_u': nrm((Ly, PEER_EXPERTS, D), D ** -0.5),
        'peer_v': nrm((Ly, PEER_EXPERTS, D), 0.5),
    }

def reference(x, c, ctx, c_ctx, w_mod, b_mod, norm1, norm2, w_in, qn_a, kn_a, sink_a, qn_b, kn_b, rpb_b,
              wa2_f, ba_f, wa2_b, ba_b, gn_c, w_oa, w_ob, w_oc, w_out, w_pq, pq_g, sub_keys, peer_u, peer_v):
    c_act = jax.nn.silu(c)
    cctx_act = jax.nn.silu(c_ctx)
    cos, sin = _axial_rope(x.shape[1])
    for i in range(DEPTH):
        p = {
            'w_mod': w_mod[i], 'b_mod': b_mod[i], 'norm1': norm1[i], 'norm2': norm2[i], 'w_in': w_in[i],
            'qn_a': qn_a[i], 'kn_a': kn_a[i], 'sink_a': sink_a[i], 'qn_b': qn_b[i], 'kn_b': kn_b[i],
            'rpb_b': rpb_b[i], 'wa2_f': wa2_f[i], 'ba_f': ba_f[i], 'wa2_b': wa2_b[i], 'ba_b': ba_b[i],
            'gn_c': gn_c[i], 'w_oa': w_oa[i], 'w_ob': w_ob[i], 'w_oc': w_oc[i], 'w_out': w_out[i],
            'w_pq': w_pq[i], 'pq_g': pq_g[i], 'sub_keys': sub_keys[i], 'peer_u': peer_u[i], 'peer_v': peer_v[i],
        }
        x, ctx = _layer(x, ctx, c_act, cctx_act, p, cos, sin, i == DEPTH - 1)
    return x


_drawn_inputs = setup_inputs


def setup_inputs(seed=0):
    import zlib

    import numpy as np

    out = dict(_drawn_inputs(seed))
    spreads = {}
    factors = {'qn_a': 8.0,
     'kn_a': 8.0,
     'sink_a': 8.0,
     'qn_b': 8.0,
     'kn_b': 8.0,
     'rpb_b': 25.275,
     'ba_f': 5.478,
     'ba_b': 5.874,
     'gn_c': 4.322}
    for name, (base, spread) in spreads.items():
        noise = np.random.default_rng([zlib.crc32(name.encode()), seed]).standard_normal(out[name].shape)
        drawn = base * np.exp(spread * noise) if base else spread * noise
        out[name] = jnp.asarray(drawn.astype(out[name].dtype))
    for name, factor in factors.items():
        out[name] = (out[name] * factor).astype(out[name].dtype)
    return out
```

```python
from contextlib import ExitStack

import numpy as np
import concourse.bass as bass
from concourse import mybir

FP = mybir.dt.float32
I32 = mybir.dt.int32
U32 = mybir.dt.uint32
ALU = mybir.AluOpType
ACT = mybir.ActivationFunctionType
AX = mybir.AxisListType

P = 128
D = 1024
KC = D // P
DEPTH = 2
SEQ, CTX = 256, 256
NT = (SEQ + CTX) // P
LT = SEQ // P
GRID_W, NA_COLS = 64, 16
HD = 64
NEG = -1e30
EPS = 1e-6
CDK, CDV, CH = 128, 256, 4
TAU = 16.0
E_KEYS, E_HEADS, TOPK = 128, 8, 16
NEXP = E_KEYS * E_KEYS
PK = E_HEADS * TOPK
RING = 3
SLOT = 4096
LEVELS = 7
GB = 8
DB = 4
HALF = D // 2
PADW = P + 1

O_KA, O_VA, O_KB, O_VB = 0, 128, 256, 768
O_KC, O_VC, O_AC = 1280, 1792, 2816
O_QA, O_QB, O_QC, O_RC, O_G = 2848, 3360, 3872, 4384, 5408

KINDS = ["mod", "norm1", "attnA", "attnB", "gla0", "gla1", "merge", "norm2", "pick", "expert"]
RUNS = [(kind, l) for l in range(DEPTH) for kind in KINDS]


def q_tiles(l):
    return NT if l < DEPTH - 1 else LT


def weight_units():
    units = []

    def add(run, name, cols, groups, engine):
        units.append(dict(run=run, name=name, layer=RUNS[run][1], cols=cols, groups=groups, engine=engine))

    for r, (kind, l) in enumerate(RUNS):
        nq = q_tiles(l)
        if kind == "mod":
            for n in range(12):
                add(r, "w_mod", (512 * n, 512), 1, "dve")
        elif kind == "attnA":
            add(r, "w_in", (O_KA, 256), NT, "act")
            add(r, "w_in", (O_QA, 512), nq, "act")
        elif kind == "attnB":
            add(r, "w_in", (O_KB, 512), NT, "act")
            add(r, "w_in", (O_QB, 512), nq, "act")
            add(r, "w_in", (O_VB, 512), NT, "act")
        elif kind in ("gla0", "gla1"):
            hp = int(kind[-1])
            add(r, "w_in", (O_AC, 32), 2, "act")
            add(r, "w_in", (O_KC + 256 * hp, 256), 2, "act")
            add(r, "w_in", (O_QC + 256 * hp, 256), 2, "act")
            add(r, "w_in", (O_VC + 512 * hp, 512), NT, "act")
            add(r, "w_in", (O_RC + 512 * hp, 512), nq, "act")
        elif kind == "merge":
            for br, name in enumerate(("w_oa", "w_ob", "w_oc")):
                for quarter in range(4):
                    add(r, name, (256 * quarter, 256), 4, "mix")
                    units[-1]["gate_col"] = O_G + D * br + 256 * quarter
            for half in range(2):
                add(r, "w_out", (512 * half, 512), nq, "dve")
        elif kind == "pick":
            add(r, "sub_keys", (0, 0), 4, "dve")
            for n in range(4):
                add(r, "w_pq", (512 * n, 512), 4, "act")
    return units


UNITS = weight_units()


def count_groups():
    order, seen = [], {"act": 0, "dve": 0}
    for u in UNITS:
        u["first"] = len(order)
        for j in range(u["groups"]):
            e = u["engine"] if u["engine"] != "mix" else ("act", "dve")[j % 2]
            seen[e] += 1
            order.append((e, seen[e]))
    loads = [0] * RING
    for n, u in enumerate(UNITS):
        u["free_after"] = u["first"] + u["groups"]
        loads[n % RING] += 2 if "gate_col" in u else 1
        u["loaded"] = 16 * loads[n % RING]
    return order


GROUPS = count_groups()
RUN_UNITS = [[n for n, u in enumerate(UNITS) if u["run"] == r] for r in range(len(RUNS))]
ATT_UNITS = {l: [(t, h) for t in range(q_tiles(l)) for h in range(8)] for l in range(DEPTH)}
CHAIN = {0: [2, 3, 0], 1: [3, 2, 1]}
ENTER = {0: {3: 0, 0: 1, 1: 2}, 1: {2: 0, 1: 1, 0: 2}}


def signals(r):
    kind, l = RUNS[r]
    nq = q_tiles(l)
    na = len(ATT_UNITS[l])
    if kind == "mod":
        return dict(mod_small=1, mod_cols=1, mod_sig=1, mod_act_in=1, mod_rows=1, mod_colT=1)
    if kind in ("norm1", "norm2"):
        n = NT if kind == "norm1" else nq
        back = 2 * n if kind == "norm2" else 0
        return dict(norm_sq=1, norm_var=1, norm_std=1, norm_x=n, norm_T=2 * n + back, norm_h=2 * n, norm_tok=back)
    if kind in ("attnA", "attnB"):
        nbias = 4 * LT if kind == "attnB" else 0
        return dict(bias_turned=nbias, bias_ready=nbias, prep_var=NT, prep_std=NT, prep_qk=NT, qk_T=NT + nq, qk_copied=NT + nq,
                    scores=na, score_max=na, probs=na, probs_T=na, probs_copied=na, heads_out=nq,
                    heads_normed=nq, heads_T=nq, heads_copied=nq)
    if kind in ("gla0", "gla1"):
        return dict(gla_z=4, gla_soft=4, gla_zfree=4, gla_ready=1,
                    gla_diff=2 + LEVELS, gla_exp=4 + LEVELS, gla_fac=4 + LEVELS, gla_sg=nq,
                    gla_kT=6, gla_kcopied=6, gla_upd=6, gla_state=6,
                    gla_att=LEVELS + 1, gla_attfree=LEVELS + 1,
                    gla_o=nq, gla_osq=nq, gla_ovar=nq, gla_ostd=nq, gla_oy=nq, gla_oT=nq, gla_ocopied=nq)
    if kind == "merge":
        return dict(gate_b=4, gate_copied=4)
    if kind == "pick":
        return dict(pk_score=16, pk_scopied=16, pk_var=1, pk_std=1, pk_top=1, pk_exp=1, pk_idx=1)
    if kind == "expert":
        return dict(gate_b=4, gate_copied=4, ex_gelu=nq, ex_stage=nq * 2 * PK // GB,
                    ex_used=nq * 2 * PK,
                    pk_top=nq - 1, pk_exp=nq - 1, pk_idx=nq - 1,
                    ex_coef=nq, ex_diag=nq * PK, ex_sums=nq * PK, ex_total=nq)
    return {}


def signal_bases():
    bases, now = [], {}
    for r in range(len(RUNS)):
        bases.append(dict(now))
        for name, n in signals(r).items():
            now[name] = now.get(name, 0) + n
    return bases, now


BASES, TOTALS = signal_bases()


def backbone(nc, t, out):
    ctx = ExitStack()
    with ctx:
        def sb(name, shape, dt=FP):
            return ctx.enter_context(nc.sbuf_tensor(name, shape, dt))

        x_sb = sb("x_sb", [P, NT, D])
        hT = sb("hT", [P, KC, NT * P])
        ring = sb("ring", [P, RING, SLOT])
        oT = sb("oT", [P, 16, NT * P])
        ident = sb("ident", [P, P])
        turn = sb("turn", [P, P])
        cos = sb("cos", [P, LT, HD])
        sin = sb("sin", [P, LT, HD])
        iota = sb("iota", [P, TOPK])
        pick_row = sb("pick_row", [2, 2, P])
        gate_rows = sb("gate_rows", [2, 2, D])
        mod_col = sb("mod_col", [P, 4, KC, 2])
        scale_col = sb("scale_col", [P, 2, KC, 2])
        params = sb("params", [P, P])
        par_col = sb("par_col", [P, 48])
        c_col = sb("c_col", [P, 2, KC])
        head_w = sb("head_w", [P, 4, HD])
        sink = sb("sink", [P, 8])
        gn = sb("gn", [P, CDV])
        ones = sb("ones", [P, 1])
        small = sb("small", [P, 16])
        arena_words = 20480
        arena = sb("arena", [P, arena_words])

        def carve():
            at = [0]

            def take(n, parts=P):
                a = at[0]
                at[0] += n
                assert at[0] <= arena_words, at[0]
                return arena[0:parts, a:a + n]
            return take

        bank = [ctx.enter_context(nc.psum_tensor(f"bank{i}", [P, 512], FP)) for i in range(8)]

        sems = {name: ctx.enter_context(nc.semaphore(name)) for name in TOTALS}
        for name in ("const_in", "phase_end", "group_done", "evac_act", "evac_dve", "dve_chain", "act_chain",
                     "stage_in", "slots_granted", "diags_granted", "out_done", "arena_in"):
            sems[name] = ctx.enter_context(nc.semaphore(name))
        ring_in = [ctx.enter_context(nc.semaphore(f"ring_in{i}")) for i in range(RING)]
        row_in = [ctx.enter_context(nc.semaphore(f"row_in{i}")) for i in range(GB)]
        S = sems

        class At:

            def __init__(self, r):
                self.base = BASES[r]

            def __call__(self, name, n):
                assert n >= 1
                return self.base.get(name, 0) + n

        def slot_view(n):
            u = UNITS[n]
            s = ring[:, n % RING, :]
            if u["name"] in ("w_in", "w_mod", "w_out", "w_pq"):
                w = u["cols"][1]
                return s[:, 0:KC * w].rearrange("p (k c) -> p k c", k=KC)
            if u["name"] == "sub_keys":
                return s[:, 0:16 * P].rearrange("p (g d) -> p g d", g=16)
            return s.rearrange("p (k c) -> p k c", k=16)

        def unit_source(n):
            u = UNITS[n]
            l = u["layer"]
            c0, w = u["cols"]
            if u["name"] in ("w_in", "w_mod", "w_out", "w_pq"):
                return t[u["name"]][l][:, c0:c0 + w].rearrange("(k p) c -> p k c", p=P)
            if u["name"] == "sub_keys":
                return t["sub_keys"][l].rearrange("h s n d -> n (h s) d")
            raise ValueError(u["name"])

        def group_bank(n, j):
            return bank[(UNITS[n]["first"] + j) % 4]

        def arena_mod():
            a = carve()
            return dict(rows=a(6144, 2), b_mod=a(6144, 2), sig=a(16))

        def arena_norm():
            a = carve()
            tok = a(NT * D).rearrange("p (t d) -> p t d", t=NT)
            return dict(tok=tok, junk=a(D), xn=a(2 * D).rearrange("p (b d) -> p b d", b=2))

        def arena_attn(br):
            a = carve()
            w = 640 if br == 0 else 1024
            kc = 1 if br == 0 else 4
            vw = 128 if br == 0 else 512
            s = dict(
                qk=a(NT * w).rearrange("p (t c) -> p t c", t=NT),
                v=a(NT * vw).rearrange("p (t c) -> p t c", t=NT),
                kT=a(kc * NT * P).rearrange("p (c t) -> p c t", c=kc),
                qT=a(4 * NT * P).rearrange("p (c t) -> p c t", c=4),
                mask=a(LT * SEQ).rearrange("p (t k) -> p t k", t=LT),
                S=a(2 * 516).rearrange("p (b k) -> p b k", b=2),
                PT=a(2 * 512).rearrange("p (b k) -> p b k", b=2),
                nmax=a(NT * 8), rsum=a(NT * 8), rinv=a(NT * 8),
                o=a(2 * 512).rearrange("p (b k) -> p b k", b=2),
                ss=a(NT * 16).rearrange("p (t h) -> p t h", t=NT),
            )
            if br == 1:
                s["bias"] = a(LT * 8 * SEQ).rearrange("p (t h k) -> p t h k", t=LT, h=8)
            s["tmp"] = a(w)
            return s

        def arena_gla():
            a = carve()

            def as_heads(z, n=NT):
                return z.rearrange("p (t h i) -> p t h i", t=n, h=2)
            flat = [a(NT * 2 * P) for _ in range(4)]
            e = [[as_heads(flat[0]), as_heads(flat[1])], [as_heads(flat[2]), as_heads(flat[3])]]
            low = arena[:, 4 * 1024:4 * 1024 + 3 * 512]
            state0 = a(3 * 512)
            aT = low[0:16, 0:2 * NT * P].rearrange("p (d t) -> p d t", d=2)
            w2 = low[0:16, 1024:1536].rearrange("p (d c) -> p d c", d=2)
            att = a(NT * 2 * PADW)
            return dict(
                k=as_heads(a(1024)), q=as_heads(a(1024)), E=e, KF=e[1], QF=[as_heads(a(1024)) for _ in range(2)],
                v=a(NT * 512).rearrange("p (t c) -> p t c", t=NT),
                r=a(NT * 512).rearrange("p (t c) -> p t c", t=NT),
                aT=aT, w2=w2,
                P=[a(NT * 2 * PADW) for _ in range(2)],
                ktok=a(2 * 256).rearrange("p (b h d) -> p b h d", b=2, h=2),
                S=[z.rearrange("p (n h v) -> p n h v", n=3, h=2) for z in (state0, a(3 * 512))],
                att=att[:, 0:1024].rearrange("p (m i) -> p m i", i=P),
                reset=att,
                dec=a(16).rearrange("p (d t h) -> p d t h", d=2, t=NT),
                ss=a(16),
                diag2=a(P),
                lvl=a(LEVELS * P).bitcast(I32).rearrange("p (l i) -> p l i", l=LEVELS),
                t1=[z[:, 0:512] for z in flat],
                t4=[z[:, 512:1024] for z in flat],
                y=flat[0].rearrange("p (b c) -> p b c", b=2),
                sg=flat[1].rearrange("p (b c) -> p b c", b=2),
                osq=flat[2],
            )

        def arena_merge():
            a = carve()
            return dict(y=a(KC * NT * P).rearrange("p (k t) -> p k t", k=KC),
                        sig=a(2 * 512).rearrange("p (b k) -> p b k", b=2),
                        tmp=a(2 * 512).rearrange("p (b k) -> p b k", b=2),
                        gb=a(2 * D).rearrange("p (s d) -> p s d", s=2))

        def junk_and_diag(z):
            return dict(junk=z.rearrange("p (b d) -> p b d", b=2),
                        diag=z[:, 0:DB * P].rearrange("p (b t) -> p b t", b=DB))

        def arena_peer():
            a = carve()
            tok, idx, gval, rstd = a(NT * D), a(NT * PK), a(NT * PK), a(64)
            rows = a(GB * D)
            return dict(tok=tok.rearrange("p (t d) -> p t d", t=NT),
                        idx=idx.bitcast(I32).rearrange("p (t k) -> p t k", t=NT),
                        gval=gval.rearrange("p (t k) -> p t k", t=NT), rstd=rstd,
                        rows=rows.rearrange("p (b d) -> p b d", b=GB),
                        skT=rows[:, 0:2048].rearrange("p (g n) -> p g n", g=16),
                        qT=rows[:, 2048:3072].rearrange("p (b k) -> p b k", b=2),
                        q2T=rows[:, 3072:4096].rearrange("p (b k) -> p b k", b=2),
                        **junk_and_diag(a(2 * D)), acc=a(D),
                        dots=a(PK), gel=a(PK), coef=a(PK), gb=a(2 * D).rearrange("p (s d) -> p s d", s=2),
                        stage=a(16).bitcast(I32),
                        s=oT[:, :, :].rearrange("p c (g n) -> p (c g) n", n=P)
                        .rearrange("p (t g) n -> p t g n", t=NT),
                        hot=hT[:, 0:4, :].rearrange("p c (m j) -> p (c m) j", j=TOPK),
                        cand=hT[:, 4:8, :].rearrange("p c (h m) -> p (c h) m", h=2),
                        tv=a(PK), tp=a(PK).bitcast(U32), gs=a(8),
                        ie=a(2 * PK).rearrange("p (w k) -> p w k", w=2),
                        sv=a(256).rearrange("p (g k) -> p g k", g=16),
                        si=a(256).bitcast(U32).rearrange("p (g k) -> p g k", g=16),
                        k12=a(256).bitcast(U32).rearrange("p (w k) -> p w k", w=2),
                        k12f=a(256).rearrange("p (w k) -> p w k", w=2))

        block = ctx.enter_context(nc.Block())

        def arena_in_count(r):
            return sum({"attnA": 1, "attnB": 17, "gla0": 5, "gla1": 5}.get(kind, 0) for kind, _ in RUNS[:r + 1])

        def meet_before(eng, r):
            if r > 0:
                eng.wait_ge(S["phase_end"], 4 * r)

        @block.sync
        def _(sp):
            for name, dst in (("ident", ident[:, :]), ("turn", turn[:, :]), ("iota", iota[:, :]),
                              ("pick_row", pick_row[:, :, :]), ("cos", cos[:, :, :]), ("sin", sin[:, :, :])):
                sp.dma_start(dst, t[name]).then_inc(S["const_in"], 16)
            for n in range(len(UNITS)):
                if n >= RING:
                    sp.wait_ge(S["group_done"], UNITS[n - RING]["free_after"])
                u = UNITS[n]
                if "gate_col" in u:
                    c0, w = u["cols"]
                    wo = t[u["name"]][u["layer"]][:, c0:c0 + w].rearrange("(k p) c -> p k c", p=P)
                    gate = t["w_in"][u["layer"]][:, u["gate_col"]:u["gate_col"] + w].rearrange("(k p) c -> p k c", p=P)
                    sp.dma_start(slot_view(n)[:, 0:KC, :], gate).then_inc(ring_in[n % RING], 16)
                    sp.dma_start(slot_view(n)[:, KC:KC + wo.shape[1], :], wo).then_inc(ring_in[n % RING], 16)
                else:
                    sp.dma_start(slot_view(n), unit_source(n)).then_inc(ring_in[n % RING], 16)
                if n == 0:
                    for i, (name, half) in enumerate((("x", 0), ("x", 1), ("ctx", 0), ("ctx", 1))):
                        sp.dma_start(x_sb[:, i, :], t[name][0][P * half:P * (half + 1), :])\
                            .then_inc(S["const_in"], 16)
            sp.wait_ge(S["phase_end"], 4 * len(RUNS))
            for i in range(LT):
                sp.dma_start(out[0][P * i:P * (i + 1), :], x_sb[:, i, :]).then_inc(S["out_done"], 16)
            sp.wait_ge(S["out_done"], 16 * LT)

        N_CONST = 10

        @block.gpsimd
        def _(pool):
            arena_loads = [0]
            for r, (kind, l) in enumerate(RUNS):
                at = At(r)
                meet_before(pool, r)
                if kind == "mod":
                    if l == 0:
                        pool.memset(params[:, :], 0.0)
                    pool.memset(ones[:, :], 1.0).then_inc(S["mod_small"], 1)
                    pool.wait_ge(S["mod_small"], at("mod_small", 1))
                    m = arena_mod()
                    pool.dma_start(m["b_mod"], bass.AP(t["b_mod"].tensor, l * 6144, [[0, 2], [1, 6144]]))\
                        .then_inc(S["stage_in"], 16)
                    for name, row, n in (("norm1", 0, 8), ("norm2", 8, 8), ("ba_f", 16, 4), ("ba_b", 20, 4),
                                         ("pq_g", 24, 1)):
                        pool.dma_start(params[row:row + n, :], t[name][l].rearrange("(k p) -> k p", p=P))\
                            .then_inc(S["stage_in"], 16)
                    pool.dma_start(params[32:40, :], t["c"][0].rearrange("(k p) -> k p", p=P))\
                        .then_inc(S["stage_in"], 16)
                    pool.dma_start(params[40:48, :], t["c_ctx"].rearrange("(k p) -> k p", p=P))\
                        .then_inc(S["stage_in"], 16)
                    for i, name in enumerate(("kn_a", "qn_a", "kn_b", "qn_b")):
                        pool.dma_start(head_w[:, i, :], bass.AP(t[name].tensor, l * HD, [[0, P], [1, HD]]))\
                            .then_inc(S["stage_in"], 16)
                    pool.dma_start(sink[:, :], bass.AP(t["sink_a"].tensor, l * 8, [[0, P], [1, 8]]))\
                        .then_inc(S["stage_in"], 16)
                    pool.dma_start(gn[:, :], bass.AP(t["gn_c"].tensor, l * CDV, [[0, P], [1, CDV]]))\
                        .then_inc(S["stage_in"], 16)
                elif kind == "attnA":
                    pool.dma_start(arena_attn(0)["mask"], t["mask_a"]).then_inc(S["arena_in"], 16)
                elif kind == "attnB":
                    a = arena_attn(1)
                    pool.dma_start(a["mask"], t["mask_b"]).then_inc(S["arena_in"], 16)
                    for qr in range(SEQ // GRID_W):
                        for kr in range(SEQ // GRID_W):
                            src = bass.AP(t["rpb_b"].tensor, l * 8 * 465 + (7 + kr - qr) * 31 + NA_COLS - GRID_W,
                                          [[1, GRID_W], [465, 8], [1, GRID_W]])
                            p0 = GRID_W * (qr % 2)
                            pool.dma_start(a["bias"][p0:p0 + GRID_W, qr // 2, :, GRID_W * kr:GRID_W * (kr + 1)], src)\
                                .then_inc(S["arena_in"], 16)
                elif kind in ("gla0", "gla1"):
                    hp = int(kind[-1])
                    g = arena_gla()
                    pool.dma_start(g["reset"], t["reset"]).then_inc(S["arena_in"], 16)
                    pool.dma_start(g["diag2"], t["diag2"]).then_inc(S["arena_in"], 16)
                    pool.dma_start(g["lvl"], t["lvl"]).then_inc(S["arena_in"], 16)
                    for d, name in enumerate(("wa2_f", "wa2_b")):
                        pool.dma_start(g["w2"][:, d, :], t[name][l][:, 256 * hp:256 * (hp + 1)])\
                            .then_inc(S["arena_in"], 16)
                elif kind == "expert":
                    e = arena_peer()
                    nq = q_tiles(l)
                    tables = [t[name].rearrange("l e d -> (l e) d") for name in ("peer_u", "peer_v")]
                    passes = [(i, table) for i in range(nq) for table in tables]
                    for ps, (i, table) in enumerate(passes):
                        if ps % 2 == 0 and i >= 1:
                            pool.wait_ge(S["pk_idx"], at("pk_idx", i))
                        with pool.Fori(0, PK // 16) as it:
                            for half in range(2):
                                first = BASES[r].get("ex_used", 0) + ps * PK + 8 * half
                                stage_n = BASES[r].get("ex_stage", 0) + ps * 16 + half + 1
                                pool.tensor_copy(e["stage"][:, 8 * half:8 * half + 8],
                                                 e["idx"][:, i, bass.ds(it * 16 + 8 * half, 8)])\
                                    .then_inc(S["ex_stage"], 1)
                                pool.wait_ge(S["ex_stage"], it * 2 + stage_n)
                                for s in range(GB):
                                    pool.wait_ge(S["ex_used"], it * 16 + (first + 1 + s))
                                    pool.sem_inc(S["slots_granted"], 1)
                                    pool.indirect_dma_start(
                                        out=e["rows"][:, s, :], out_offset=None, in_=table,
                                        in_offset=bass.IndirectOffsetOnAxis(
                                            ap=e["stage"][:, 8 * half + s:8 * half + s + 1], axis=0),
                                    ).then_inc(row_in[s], 16)
                pool.drain().then_inc(S["phase_end"], 1)

        @block.tensor
        def _(pe):
            def open_group(n, j):
                if j == 0:
                    pe.wait_ge(ring_in[n % RING], UNITS[n]["loaded"])
                g = UNITS[n]["first"] + j
                if g >= 4:
                    engine, count = GROUPS[g - 4]
                    pe.wait_ge(S["evac_" + engine], count)
                return group_bank(n, j)

            def tokens_major(n, w, tiles):
                sv = slot_view(n)
                for i in range(tiles):
                    b = open_group(n, i)
                    for k in range(KC):
                        m = nc.tensor.matmul(b[:, 0:w], hT[:, k, P * i:P * (i + 1)], sv[:, k, 0:w],
                                             start=(k == 0), stop=(k == KC - 1))
                    m.then_inc(S["group_done"], 1)

            def features_major(n, j, c0, w, src, tokens):
                sv = slot_view(n)
                b = open_group(n, j)
                for k in range(KC):
                    m = nc.tensor.matmul(b[0:w, 0:tokens], sv[:, k, c0:c0 + w], src[:, k, 0:tokens],
                                         start=(k == 0), stop=(k == KC - 1))
                return m

            for r, (kind, l) in enumerate(RUNS):
                at = At(r)
                nq = q_tiles(l)
                nq_tok = nq * P
                units = RUN_UNITS[r]
                meet_before(pe, r)
                if kind == "mod":
                    m = arena_mod()
                    if l == 0:
                        pe.wait_ge(S["const_in"], 16 * N_CONST)
                    pe.wait_ge(S["stage_in"], 16 * 14 * (l + 1))
                    nc.tensor.transpose(bank[4][:, 0:P], params[:, :], ident[:, :]).then_inc(S["mod_cols"], 1)
                    pe.wait_ge(S["mod_act_in"], at("mod_act_in", 1))
                    for j, n in enumerate(units):
                        sv = slot_view(n)
                        b = open_group(n, 0)
                        for k in range(KC):
                            last = nc.tensor.matmul(b[0:2, :], c_col[:, :, k], sv[:, k, :],
                                                    start=(k == 0), stop=(k == KC - 1))
                        last.then_inc(S["group_done"], 1)
                    pe.wait_ge(S["mod_rows"], at("mod_rows", 1))
                    for i, kd in enumerate((0, 1, 3, 4)):
                        for k in range(KC):
                            c0 = kd * D + k * P
                            o = 2 * (i * KC + k)
                            last = nc.tensor.matmul(bank[5][:, o:o + 2], m["rows"][:, c0:c0 + P],
                                                    ident[0:2, 0:2], start=True, stop=True)
                    last.then_inc(S["mod_colT"], 1)
                elif kind in ("norm1", "norm2"):
                    a = arena_norm()
                    n = NT if kind == "norm1" else nq
                    for i in range(n):
                        pe.wait_ge(S["norm_x"], at("norm_x", i + 1))
                        for half in range(2):
                            j = 2 * i + half
                            if j >= 4:
                                pe.wait_ge(S["norm_h"], at("norm_h", j - 3))
                            for c in range(4):
                                k = 4 * half + c
                                last = nc.tensor.transpose(bank[4 + j % 4][:, P * c:P * (c + 1)],
                                                           a["xn"][:, i % 2, P * k:P * (k + 1)], ident[:, :])
                            last.then_inc(S["norm_T"], 1)
                    if kind == "norm2":
                        pe.wait_ge(S["norm_h"], at("norm_h", 2 * n))
                        for i in range(n):
                            for half in range(2):
                                j = 2 * i + half
                                if j >= 4:
                                    pe.wait_ge(S["norm_tok"], at("norm_tok", j - 3))
                                for c in range(4):
                                    k = 4 * half + c
                                    last = nc.tensor.transpose(bank[4 + j % 4][:, P * c:P * (c + 1)],
                                                               hT[:, k, P * i:P * (i + 1)], ident[:, :])
                                last.then_inc(S["norm_T"], 1)
                elif kind in ("attnA", "attnB"):
                    br = 0 if kind == "attnA" else 1
                    a = arena_attn(br)
                    kw = 128 if br == 0 else 512
                    kc = kw // P
                    tokens_major(units[0], 256 if br == 0 else 512, NT)
                    tokens_major(units[1], 512, nq)
                    if br == 1:
                        tokens_major(units[2], 512, NT)
                    if br == 1:
                        pe.wait_ge(S["arena_in"], 16 * arena_in_count(r))
                        for j in range(4 * LT):
                            if j >= 4:
                                pe.wait_ge(S["bias_ready"], at("bias_ready", j - 3))
                            nc.tensor.matmul(bank[4 + j % 4][:, :], turn[:, :],
                                             a["bias"][:, j // 4, 2 * (j % 4):2 * (j % 4) + 2, :], start=True, stop=True)\
                                .then_inc(S["bias_turned"], 1)
                        pe.wait_ge(S["bias_ready"], at("bias_ready", 4 * LT))
                    j = 0
                    for i in range(NT):
                        pe.wait_ge(S["prep_qk"], at("prep_qk", i + 1))
                        for part in range(2 if i < nq else 1):
                            if j >= 4:
                                pe.wait_ge(S["qk_copied"], at("qk_copied", j - 3))
                            b = bank[4 + j % 4]
                            for c in range(kc if part == 0 else 4):
                                q0 = 0 if part == 0 else kw
                                src = a["qk"][:, i, q0 + P * c:q0 + P * (c + 1)]
                                last = nc.tensor.transpose(b[:, P * c:P * (c + 1)], src, ident[:, :])
                            last.then_inc(S["qk_T"], 1)
                            j += 1
                    pe.wait_ge(S["qk_copied"], at("qk_copied", j))

                    def scores(u):
                        i, h = ATT_UNITS[l][u]
                        half, qc = (h // 4, h % 4) if br == 0 else (h % 2, h // 2)
                        kch = 0 if br == 0 else qc
                        lo = 0 if i < LT else SEQ
                        rows = slice(HD * half, HD * (half + 1))
                        if u >= 2:
                            pe.wait_ge(S["score_max"], at("score_max", u - 1))
                        nc.tensor.matmul(bank[4 + u % 2][:, lo:SEQ + CTX], a["qT"][rows, qc, P * i:P * (i + 1)],
                                         a["kT"][rows, kch, lo:SEQ + CTX], start=True, stop=True)\
                            .then_inc(S["scores"], 1)

                    def values(u):
                        i, h = ATT_UNITS[l][u]
                        c0 = 0 if i < LT else LT
                        vc = HD * (h // 4) if br == 0 else HD * h
                        pe.wait_ge(S["probs_copied"], at("probs_copied", u + 1))
                        if h == 0 and i >= 2:
                            pe.wait_ge(S["heads_normed"], at("heads_normed", i - 1))
                        ob = bank[2 + i % 2]
                        for c in range(c0, NT):
                            last = nc.tensor.matmul(ob[:, HD * h:HD * (h + 1)], a["PT"][:, u % 2, P * c:P * (c + 1)],
                                                    a["v"][:, c, vc:vc + HD], start=(c == c0), stop=(c == NT - 1))
                        if h == 7:
                            last.then_inc(S["heads_out"], 1)

                    def out_T(i):
                        pe.wait_ge(S["heads_normed"], at("heads_normed", i + 1))
                        if i >= 2:
                            pe.wait_ge(S["heads_copied"], at("heads_copied", i - 1))
                        for c in range(4):
                            last = nc.tensor.transpose(bank[i % 2][:, P * c:P * (c + 1)],
                                                       a["o"][:, i % 2, P * c:P * (c + 1)], ident[:, :])
                        last.then_inc(S["heads_T"], 1)

                    nu = len(ATT_UNITS[l])
                    scores(0)
                    for u in range(nu):
                        if u + 1 < nu:
                            scores(u + 1)
                        i, h = ATT_UNITS[l][u]
                        pe.wait_ge(S["probs"], at("probs", u + 1))
                        if u >= 2:
                            pe.wait_ge(S["probs_copied"], at("probs_copied", u - 1))
                        for c in range(0 if i < LT else LT, NT):
                            last = nc.tensor.transpose(bank[6 + u % 2][:, P * c:P * (c + 1)],
                                                       a["S"][:, u % 2, P * c:P * (c + 1)], ident[:, :])
                        last.then_inc(S["probs_T"], 1)
                        if u >= 1:
                            values(u - 1)
                        if h == 2 and i >= 1:
                            out_T(i - 1)
                    values(nu - 1)
                    out_T(nq - 1)
                elif kind in ("gla0", "gla1"):
                    g = arena_gla()
                    ua, uk, uq, uv, ur = units
                    for d in range(2):
                        features_major(ua, d, 16 * d, 16, hT, NT * P).then_inc(S["group_done"], 1)
                    for hh in range(2):
                        features_major(uk, hh, P * hh, P, hT, NT * P).then_inc(S["group_done"], 1)
                    for d in range(2):
                        pe.wait_ge(S["evac_act"], GROUPS[UNITS[ua]["first"] + 1][1])
                        if d == 0:
                            pe.wait_ge(S["arena_in"], 16 * arena_in_count(r))
                        for hh in range(2):
                            nc.tensor.matmul(bank[4 + 2 * d + hh][:, :], g["w2"][:, d, P * hh:P * (hh + 1)],
                                             g["aT"][:, d, :], start=True, stop=True).then_inc(S["gla_z"], 1)
                    for hh in range(2):
                        features_major(uq, hh, P * hh, P, hT, nq_tok).then_inc(S["group_done"], 1)
                    tokens_major(uv, 512, NT)
                    tokens_major(ur, 512, nq)

                    pe.wait_ge(S["gla_zfree"], at("gla_zfree", 4))
                    steps = [(d, s) for s in range(3) for d in range(2)]

                    def key_T(n):
                        d, s = steps[n]
                        i = CHAIN[d][s]
                        if n == 0:
                            pe.wait_ge(S["gla_fac"], at("gla_fac", 2))
                        if n >= 2:
                            pe.wait_ge(S["gla_kcopied"], at("gla_kcopied", n - 1))
                        for hh in range(2):
                            last = nc.tensor.transpose(bank[4 + n % 2][:, P * hh:P * (hh + 1)],
                                                       g["KF"][d][:, i, hh, :], ident[:, :])
                        last.then_inc(S["gla_kT"], 1)

                    key_T(0)
                    for n, (d, s) in enumerate(steps):
                        if n + 1 < len(steps):
                            key_T(n + 1)
                        i = CHAIN[d][s]
                        pe.wait_ge(S["gla_kcopied"], at("gla_kcopied", n + 1))
                        if n == 0:
                            pe.wait_ge(S["evac_act"], GROUPS[UNITS[uv]["first"] + NT - 1][1])
                        if n >= 2:
                            pe.wait_ge(S["gla_state"], at("gla_state", n - 1))
                        for hh in range(2):
                            last = nc.tensor.matmul(bank[6 + n % 2][:, CDV * hh:CDV * (hh + 1)],
                                                    g["ktok"][:, n % 2, hh, :], g["v"][:, i, CDV * hh:CDV * (hh + 1)],
                                                    start=True, stop=True)
                        last.then_inc(S["gla_upd"], 1)
                    pe.wait_ge(S["gla_state"], at("gla_state", 6))

                    per = 4
                    nb = nq * 2 // per
                    for lv in range(LEVELS + 1):
                        if lv >= 1:
                            pe.wait_ge(S["gla_fac"], at("gla_fac", 4 + lv))
                        if lv >= 2:
                            pe.wait_ge(S["gla_attfree"], at("gla_attfree", lv - 1))
                        kk, qq = (g["k"], g["q"]) if lv == 0 else (g["E"][(lv - 1) % 2][1], g["E"][(lv - 1) % 2][0])
                        for i in range(nq):
                            for hh in range(2):
                                m = 2 * i + hh
                                b = bank[4 + 2 * (lv % 2) + m // per]
                                c = m % per
                                last = nc.tensor.matmul(b[:, P * c:P * (c + 1)], kk[:, i, hh, :], qq[:, i, hh, :],
                                                        start=True, stop=True)
                        last.then_inc(S["gla_att"], 1)
                    pe.wait_ge(S["gla_attfree"], at("gla_attfree", LEVELS + 1))

                    def o_T(i):
                        pe.wait_ge(S["gla_oy"], at("gla_oy", i + 1))
                        if i >= 2:
                            pe.wait_ge(S["gla_ocopied"], at("gla_ocopied", i - 1))
                        for c in range(4):
                            last = nc.tensor.transpose(bank[i % 2][:, P * c:P * (c + 1)],
                                                       g["y"][:, i % 2, P * c:P * (c + 1)], ident[:, :])
                        last.then_inc(S["gla_oT"], 1)

                    for i in range(nq):
                        for hh in range(2):
                            terms = [(g["att"][:, 2 * i + hh, :], g["v"][:, i, CDV * hh:CDV * (hh + 1)])]
                            for d in range(2):
                                if i in ENTER[d]:
                                    terms.append((g["QF"][d][:, i, hh, :], g["S"][d][:, ENTER[d][i], hh, :]))
                            for m, (lhs, rhs) in enumerate(terms):
                                last = nc.tensor.matmul(bank[4 + i][:, CDV * hh:CDV * (hh + 1)], lhs, rhs,
                                                        start=(m == 0), stop=(m == len(terms) - 1))
                        last.then_inc(S["gla_o"], 1)
                    for i in range(nq):
                        o_T(i)
                elif kind == "merge":
                    a = arena_merge()
                    u = list(units)
                    for c0, ks in ((0, 4), (4, 4), (8, 8)):
                        for quarter in range(4):
                            n = u.pop(0)
                            for c in range(2):
                                features_major(n, 2 * c, P * c, P, hT, nq_tok).then_inc(S["group_done"], 1)
                                b = open_group(n, 2 * c + 1)
                                for k in range(ks):
                                    last = nc.tensor.matmul(b[:, 0:nq_tok], slot_view(n)[:, KC + k, P * c:P * (c + 1)],
                                                            oT[:, c0 + k, 0:nq_tok], start=(k == 0),
                                                            stop=(k == ks - 1))
                                last.then_inc(S["group_done"], 1)
                    for s in range(2):
                        for half in range(2):
                            nc.tensor.matmul(bank[4 + 2 * s + half][:, :], pick_row[:, s, :],
                                             gate_rows[:, 0, 512 * half:512 * (half + 1)], start=True, stop=True)\
                                .then_inc(S["gate_b"], 1)
                    n_last = u[0] - 1
                    pe.wait_ge(S["evac_dve"], GROUPS[UNITS[n_last]["first"] + 3][1])
                    for n in u:
                        sv = slot_view(n)
                        for i in range(nq):
                            b = open_group(n, i)
                            for k in range(KC):
                                last = nc.tensor.matmul(b[:, :], a["y"][:, k, P * i:P * (i + 1)], sv[:, k, :],
                                                        start=(k == 0), stop=(k == KC - 1))
                            last.then_inc(S["group_done"], 1)
                elif kind == "pick":
                    a = arena_peer()
                    us, upq = units[0], units[1:]
                    sv = slot_view(us)
                    for j in range(4):
                        b = open_group(us, j)
                        for c in range(4):
                            last = nc.tensor.transpose(b[:, P * c:P * (c + 1)], sv[:, 4 * j + c, :], ident[:, :])
                        last.then_inc(S["group_done"], 1)

                    def score(gr):
                        n, j = upq[gr // 4], gr % 4
                        pe.wait_ge(S["evac_act"], GROUPS[UNITS[n]["first"] + j][1])
                        if gr == 0:
                            pe.wait_ge(S["evac_dve"], GROUPS[UNITS[us]["first"] + 3][1])
                        if gr >= 3:
                            pe.wait_ge(S["pk_scopied"], at("pk_scopied", gr - 2))
                        for i in range(nq):
                            nc.tensor.matmul(bank[7][:, gr * nq + i:gr * nq + i + 1],
                                             a["q2T"][:, gr % 2, P * i:P * (i + 1)], ones[:, :],
                                             start=True, stop=True)
                            last = nc.tensor.matmul(bank[4 + gr % 3][:, P * i:P * (i + 1)],
                                                    a["qT"][:, gr % 2, P * i:P * (i + 1)], a["skT"][:, gr, :],
                                                    start=True, stop=True)
                        last.then_inc(S["pk_score"], 1)

                    for gr in range(16):
                        features_major(upq[gr // 4], gr % 4, P * (gr % 4), P, hT, nq_tok)\
                            .then_inc(S["group_done"], 1)
                        if gr >= 1:
                            score(gr - 1)
                    score(15)
                elif kind == "expert":
                    for s in range(2):
                        for half in range(2):
                            nc.tensor.matmul(bank[4 + 2 * s + half][:, :], pick_row[:, s, :],
                                             gate_rows[:, 1, 512 * half:512 * (half + 1)], start=True, stop=True)\
                                .then_inc(S["gate_b"], 1)
                    e = arena_peer()
                    if l == 0:
                        pe.sem_inc(S["ex_sums"], DB)
                    used0 = BASES[r].get("ex_used", 0)
                    for i in range(nq):
                        pe.wait_ge(S["ex_coef"], at("ex_coef", i + 1))
                        zero = e["acc"][0:2, 0:HALF]
                        nc.tensor.matmul(bank[i % 2][:, :], zero[:, 0:P], zero, start=True, stop=False)
                        with pe.Fori(0, PK // 16) as it:
                            for n in range(16):
                                s = n % GB
                                pe.wait_ge(row_in[s], it * 32 + 16 * (used0 // GB + (2 * i + 1) * (PK // GB) + n // GB + 1))
                                pe.wait_ge(S["ex_diag"], it * 16 + at("ex_diag", i * PK + n + 1))
                                nc.tensor.matmul(bank[i % 2][:, :], e["diag"][:, n % DB, :], e["rows"][:, s, 0:HALF],
                                                 start=False, stop=False).then_inc(S["ex_sums"], 1)
                        nc.tensor.matmul(bank[i % 2][:, :], zero[:, 0:P], zero, start=False, stop=True)\
                            .then_inc(S["ex_total"], 1)
                pe.drain().then_inc(S["phase_end"], 1)

        def gla_out_copy(act, g, at, i, hp):
            act.wait_ge(S["gla_oT"], at("gla_oT", i + 1))
            nc.scalar.copy(oT[:, 8 + 4 * hp:12 + 4 * hp, P * i:P * (i + 1)],
                           bank[i % 2][:, :].rearrange("p (c t) -> p c t", c=4)).then_inc(S["gla_ocopied"], 1)

        @block.scalar
        def _(act):
            chain = [0]

            def link(ins):
                chain[0] += 1
                ins.then_inc(S["act_chain"], 1)
                act.wait_ge(S["act_chain"], chain[0])

            def wait_group(n, j):
                act.wait_ge(S["group_done"], UNITS[n]["first"] + j + 1)
                return group_bank(n, j)

            for r, (kind, l) in enumerate(RUNS):
                at = At(r)
                nq = q_tiles(l)
                units = RUN_UNITS[r]
                meet_before(act, r)
                if kind == "mod":
                    m = arena_mod()
                    act.wait_ge(S["mod_cols"], at("mod_cols", 1))
                    nc.scalar.activation(m["sig"], bank[4][:, 32:48], ACT.Sigmoid).then_inc(S["mod_sig"], 1)
                elif kind in ("norm1", "norm2"):
                    a = arena_norm()
                    n = NT if kind == "norm1" else nq
                    for i in range(n):
                        last = nc.scalar.activation(a["junk"], x_sb[:, i, :], ACT.Square,
                                                    accum_out=small[:, i:i + 1])
                        if i < n - 1:
                            link(last)
                    last.then_inc(S["norm_sq"], 1)
                    act.wait_ge(S["norm_var"], at("norm_var", 1))
                    nc.scalar.activation(small[:, 8:8 + n], small[:, 4:4 + n], ACT.Sqrt).then_inc(S["norm_std"], 1)
                    if kind == "norm2":
                        for j in range(2 * n):
                            act.wait_ge(S["norm_T"], at("norm_T", 2 * n + j + 1))
                            nc.scalar.copy(a["tok"][:, j // 2, 512 * (j % 2):512 * (j % 2) + 512],
                                           bank[4 + j % 4][:, :]).then_inc(S["norm_tok"], 1)
                elif kind in ("attnA", "attnB"):
                    br = 0 if kind == "attnA" else 1
                    a = arena_attn(br)
                    kw = 128 if br == 0 else 512
                    kc = kw // P
                    for i in range(NT):
                        b = wait_group(units[0], i)
                        if br == 0:
                            nc.scalar.copy(a["v"][:, i, :], b[:, 128:256])
                        nc.scalar.copy(a["qk"][:, i, 0:kw], b[:, 0:kw]).then_inc(S["evac_act"], 1)
                    for i in range(nq):
                        b = wait_group(units[1], i)
                        q, b = a["qk"][:, i, kw:kw + 512], b[:, :]
                        if br == 0:
                            q = q.rearrange("p (j s d) -> p j s d", j=4, s=2)
                            b = b.rearrange("p (s j d) -> p j s d", s=2, j=4)
                        nc.scalar.copy(q, b).then_inc(S["evac_act"], 1)
                    for i in range(NT):
                        act.wait_ge(S["prep_var"], at("prep_var", i + 1))
                        nh = (kw + (512 if i < nq else 0)) // HD
                        nc.scalar.activation(a["ss"][:, i, 0:nh], a["ss"][:, i, 0:nh], ACT.Sqrt).then_inc(S["prep_std"], 1)
                    if br == 1:
                        for i in range(NT):
                            b = wait_group(units[2], i)
                            nc.scalar.copy(a["v"][:, i, :], b[:, :]).then_inc(S["evac_act"], 1)
                    j = 0
                    for i in range(NT):
                        for part in range(2 if i < nq else 1):
                            act.wait_ge(S["qk_T"], at("qk_T", j + 1))
                            c = kc if part == 0 else 4
                            dst = a["kT" if part == 0 else "qT"][:, 0:c, P * i:P * (i + 1)]
                            nc.scalar.copy(dst, bank[4 + j % 4][:, 0:P * c].rearrange("p (c t) -> p c t", c=c))\
                                .then_inc(S["qk_copied"], 1)
                            j += 1
                    nu = len(ATT_UNITS[l])

                    def copy_T(u):
                        i, h = ATT_UNITS[l][u]
                        lo = 0 if i < LT else SEQ
                        act.wait_ge(S["probs_T"], at("probs_T", u + 1))
                        nc.scalar.copy(a["PT"][:, u % 2, lo:512], bank[6 + u % 2][:, lo:512])\
                            .then_inc(S["probs_copied"], 1)
                        if h == 4 and i >= 1:
                            out_copy(i - 1)

                    def out_copy(i):
                        act.wait_ge(S["heads_T"], at("heads_T", i + 1))
                        nc.scalar.copy(oT[:, 4 * br:4 * br + 4, P * i:P * (i + 1)],
                                       bank[i % 2][:, :].rearrange("p (c t) -> p c t", c=4))\
                            .then_inc(S["heads_copied"], 1)

                    for u in range(nu):
                        i, h = ATT_UNITS[l][u]
                        lo = 0 if i < LT else SEQ
                        hi = 513 if br == 0 else 512
                        act.wait_ge(S["score_max"], at("score_max", u + 1))
                        c = 8 * i + h
                        nc.scalar.activation(a["S"][:, u % 2, lo:hi], a["S"][:, u % 2, lo:hi], ACT.Exp,
                                             bias=a["nmax"][:, c:c + 1], accum_out=a["rsum"][:, c:c + 1])\
                            .then_inc(S["probs"], 1)
                        if u >= 1:
                            copy_T(u - 1)
                    copy_T(nu - 1)
                    out_copy(nq - 1)
                elif kind in ("gla0", "gla1"):
                    hp = int(kind[-1])
                    g = arena_gla()
                    ua, uk, uq, uv, ur = units
                    for d in range(2):
                        b = wait_group(ua, d)
                        nc.scalar.copy(g["aT"][:, d, :], b[0:16, :]).then_inc(S["evac_act"], 1)
                    for hh in range(2):
                        b = wait_group(uk, hh)
                        nc.scalar.copy(g["k"][:, :, hh, :], b[:, :].rearrange("p (t i) -> p t i", t=NT))\
                            .then_inc(S["evac_act"], 1)
                    for j in range(4):
                        d, hh = divmod(j, 2)
                        act.wait_ge(S["gla_z"], at("gla_z", j + 1))
                        c = 16 + 4 * d + 2 * hp + hh
                        link(nc.scalar.activation(g["t1"][j], bank[4 + j][:, :], ACT.Abs, bias=par_col[:, c:c + 1]))
                        link(nc.scalar.activation(g["t1"][j], g["t1"][j], ACT.Exp, scale=-1.0))
                        nc.scalar.activation(g["t1"][j], g["t1"][j], ACT.Ln, bias=1.0).then_inc(S["gla_soft"], 1)
                    for hh in range(2):
                        b = wait_group(uq, hh)
                        nc.scalar.mul(g["q"][:, 0:nq, hh, :], b[:, 0:nq * P].rearrange("p (t i) -> p t i", t=nq),
                                      CDK ** -0.5).then_inc(S["evac_act"], 1)
                    for i in range(NT):
                        b = wait_group(uv, i)
                        nc.scalar.copy(g["v"][:, i, :], b[:, :]).then_inc(S["evac_act"], 1)
                    for i in range(nq):
                        b = wait_group(ur, i)
                        nc.scalar.copy(g["r"][:, i, :], b[:, :]).then_inc(S["evac_act"], 1)
                    Pv = [z.rearrange("p (t h i) -> p t h i", t=NT, h=2) for z in g["P"]]
                    act.wait_ge(S["gla_ready"], at("gla_ready", 1))
                    sc = 1.0 / TAU
                    for d in range(2):
                        nc.scalar.activation(g["dec"][:, d, :, :], Pv[d][:, :, :, P:P + 1].rearrange("p t h o -> p t (h o)"), ACT.Exp, scale=sc)
                    nc.scalar.activation(g["KF"][1][:, :, :, :], Pv[1][:, :, :, 0:P], ACT.Exp, scale=sc)\
                        .then_inc(S["gla_exp"], 1)
                    nc.scalar.activation(g["QF"][0][:, 0:nq, :, :], Pv[0][:, 0:nq, :, 1:PADW], ACT.Exp, scale=sc)\
                        .then_inc(S["gla_exp"], 1)
                    act.wait_ge(S["gla_diff"], at("gla_diff", 1))
                    nc.scalar.activation(g["KF"][0][:, :, :, :], g["KF"][0][:, :, :, :], ACT.Exp, scale=sc)\
                        .then_inc(S["gla_exp"], 1)
                    act.wait_ge(S["gla_diff"], at("gla_diff", 2))
                    nc.scalar.activation(g["QF"][1][:, 0:nq, :, :], g["QF"][1][:, 0:nq, :, :], ACT.Exp, scale=sc)\
                        .then_inc(S["gla_exp"], 1)

                    def key_copy(n):
                        act.wait_ge(S["gla_kT"], at("gla_kT", n + 1))
                        if n >= 2:
                            act.wait_ge(S["gla_upd"], at("gla_upd", n - 1))
                        nc.scalar.copy(g["ktok"][:, n % 2, :, :],
                                       bank[4 + n % 2][:, 0:256].rearrange("p (h d) -> p h d", h=2))\
                            .then_inc(S["gla_kcopied"], 1)
                    for n in range(6):
                        key_copy(n)
                    for lv in range(LEVELS):
                        act.wait_ge(S["gla_diff"], at("gla_diff", 3 + lv))
                        eq, ek = g["E"][lv % 2]
                        nc.scalar.activation(eq[:, 0:nq, :, :], eq[:, 0:nq, :, :], ACT.Exp, scale=sc)
                        nc.scalar.activation(ek[:, 0:nq, :, :], ek[:, 0:nq, :, :], ACT.Exp, scale=sc)\
                            .then_inc(S["gla_exp"], 1)
                    for i in range(nq):
                        act.wait_ge(S["gla_o"], at("gla_o", i + 1))
                        for hh in range(2):
                            last = nc.scalar.activation(g["osq"][:, CDV * hh:CDV * (hh + 1)],
                                                        bank[4 + i][:, CDV * hh:CDV * (hh + 1)], ACT.Square,
                                                        accum_out=g["ss"][:, 2 * i + hh:2 * i + hh + 1])
                        if i < nq - 1:
                            last.then_inc(S["gla_osq"], 1)
                            act.wait_ge(S["gla_osq"], at("gla_osq", i + 1))
                        else:
                            last.then_inc(S["gla_osq"], 1)
                    for i in range(nq):
                        act.wait_ge(S["gla_ovar"], at("gla_ovar", i + 1))
                        nc.scalar.activation(g["ss"][:, 8 + 2 * i:10 + 2 * i], g["ss"][:, 8 + 2 * i:10 + 2 * i],
                                             ACT.Sqrt).then_inc(S["gla_ostd"], 1)
                    for i in range(nq):
                        if i >= 2:
                            act.wait_ge(S["gla_oy"], at("gla_oy", i - 1))
                        nc.scalar.activation(g["sg"][:, i % 2, :], g["r"][:, i, :], ACT.Sigmoid)\
                            .then_inc(S["gla_sg"], 1)
                        if i >= 1:
                            gla_out_copy(act, g, at, i - 1, hp)
                    gla_out_copy(act, g, at, nq - 1, hp)
                elif kind == "merge":
                    a = arena_merge()
                    u = [n for n in units if UNITS[n]["engine"] == "mix"]
                    m = 0
                    for n in u:
                        for c in range(2):
                            b = wait_group(n, 2 * c)
                            if m >= 2:
                                act.wait_ge(S["evac_dve"], GROUPS[UNITS[u[(m - 2) // 2]]["first"] + 2 * ((m - 2) % 2) + 1][1])
                            nc.scalar.activation(a["sig"][:, m % 2, 0:nq * P], b[:, 0:nq * P], ACT.Sigmoid)\
                                .then_inc(S["evac_act"], 1)
                            m += 1
                elif kind == "pick":
                    a = arena_peer()
                    for gr in range(16):
                        b = wait_group(units[1 + gr // 4], gr % 4)
                        if gr >= 2:
                            act.wait_ge(S["pk_score"], at("pk_score", gr - 1))
                        nc.scalar.activation(a["q2T"][:, gr % 2, 0:nq * P], b[:, 0:nq * P], ACT.Square)
                        nc.scalar.copy(a["qT"][:, gr % 2, 0:nq * P], b[:, 0:nq * P]).then_inc(S["evac_act"], 1)
                    act.wait_ge(S["pk_var"], at("pk_var", 1))
                    rstd = a["rstd"].rearrange("p (g t) -> p g t", t=NT)[:, :, 0:nq]
                    nc.scalar.activation(rstd, rstd, ACT.Sqrt).then_inc(S["pk_std"], 1)
                    act.wait_ge(S["pk_top"], at("pk_top", 1))
                    nc.scalar.activation(a["gval"][:, 0, :], a["gval"][:, 0, :], ACT.Exp).then_inc(S["pk_exp"], 1)
                elif kind == "expert":
                    e = arena_peer()
                    for i in range(nq):
                        act.wait_ge(S["ex_used"], at("ex_used", GB + (2 * i + 1) * PK))
                        nc.scalar.activation(e["gel"], e["dots"], ACT.Gelu).then_inc(S["ex_gelu"], 1)
                        act.wait_ge(S["ex_coef"], at("ex_coef", i + 1))
                        with act.Fori(0, PK // 16) as it:
                            for n in range(16):
                                act.wait_ge(S["ex_sums"], it * 16 + at("ex_sums", i * PK + n + 1))
                                act.sem_inc(S["diags_granted"], 1)
                                nc.scalar.activation(e["diag"][:, n % DB, :], ident[:, :], ACT.Identity,
                                                     scale=e["coef"][:, bass.ds(it * 16 + n, 1)])\
                                    .then_inc(S["ex_diag"], 1)
                        if i + 1 < nq:
                            act.wait_ge(S["pk_top"], at("pk_top", i + 1))
                            nc.scalar.activation(e["gval"][:, i + 1, :], e["gval"][:, i + 1, :], ACT.Exp)\
                                .then_inc(S["pk_exp"], 1)
                act.drain().then_inc(S["phase_end"], 1)

        def top16(rows, link):
            v = nc.vector
            for z, val, _ in rows:
                last = v.max(val[:, 0:8], z)
            link(last)
            for z, val, place in rows:
                v.max_index(place[:, 0:8], val[:, 0:8], z)
            for z, val, _ in rows:
                last = v.match_replace(z, val[:, 0:8], z, -3.0e38)
            link(last)
            for z, val, _ in rows:
                last = v.max(val[:, 8:16], z)
            link(last)
            for z, val, place in rows:
                last = v.max_index(place[:, 8:16], val[:, 8:16], z)
            link(last)

        @block.vector
        def _(dve):
            chain = [0]
            v = nc.vector

            def link(ins):
                chain[0] += 1
                ins.then_inc(S["dve_chain"], 1)
                dve.wait_ge(S["dve_chain"], chain[0])

            def signal(ins, name, at, n):
                ins.then_inc(S[name], 1)
                dve.wait_ge(S[name], at(name, n))

            def wait_group(n, j):
                dve.wait_ge(S["group_done"], UNITS[n]["first"] + j + 1)
                return group_bank(n, j)

            def evac_count(n, j):
                return GROUPS[UNITS[n]["first"] + j][1]

            def choose(i, part, l, at, n):
                a = arena_peer()
                s, sv, si, tv, tp = a["s"][:, i, :, :], a["sv"], a["si"], a["tv"], a["tp"]
                lists = sv.rearrange("p (h w) k -> p h w k", w=2)
                tv3 = tv.rearrange("p (h k) -> p h k", h=E_HEADS)
                g3 = a["gval"][:, i, :].rearrange("p (h k) -> p h k", h=E_HEADS)
                if part < 3:
                    top16([(s[:, gr, :], sv[:, gr, :], si[:, gr, :]) for gr in range(6 * part, min(6 * part + 6, 16))],
                          link)
                if part == 2:
                    rstd = a["rstd"].rearrange("p (g t) -> p g t", t=NT)
                    link(v.tensor_tensor(sv, sv, rstd[:, :, i:i + 1].broadcast_to([P, 16, TOPK]), ALU.mult))
                    c4 = a["cand"].rearrange("p h (j k) -> p h j k", k=TOPK)
                    link(v.tensor_tensor(c4, lists[:, :, 0, :].unsqueeze(3).broadcast_to([P, E_HEADS, TOPK, TOPK]),
                                         lists[:, :, 1, :].unsqueeze(2).broadcast_to([P, E_HEADS, TOPK, TOPK]),
                                         ALU.add))
                elif part in (3, 4):
                    top16([(a["cand"][:, h, :], tv[:, TOPK * h:TOPK * (h + 1)], tp[:, TOPK * h:TOPK * (h + 1)])
                           for h in range(4 * (part - 3), 4 * (part - 2))], link)
                elif part == 5:
                    v.tensor_tensor(g3, tv3, tv3[:, :, 0:1].broadcast_to([P, E_HEADS, TOPK]), ALU.subtract)\
                        .then_inc(S["pk_top"], 1)
                    v.tensor_scalar(a["k12"][:, 0, :], tp, 4, None, ALU.logical_shift_right)
                    v.tensor_scalar(a["k12"][:, 1, :], tp, TOPK - 1, None, ALU.bitwise_and)
                    link(v.tensor_copy(sv, si))
                    link(v.tensor_copy(a["k12f"], a["k12"]))
                elif part in (6, 7):
                    w = part - 6
                    link(v.tensor_tensor(a["hot"], a["k12f"][:, w, :].unsqueeze(2).broadcast_to([P, PK, TOPK]),
                                         iota[:, :].unsqueeze(1).broadcast_to([P, PK, TOPK]), ALU.is_equal))
                    h4 = a["hot"].rearrange("p (h k) j -> p h k j", h=E_HEADS)
                    link(v.tensor_tensor(h4, h4, lists[:, :, w, :].unsqueeze(2)
                                         .broadcast_to([P, E_HEADS, TOPK, TOPK]), ALU.mult))
                    link(v.tensor_reduce(a["ie"][:, w, :], a["hot"], AX.X, ALU.add))
                if part == 7:
                    link(v.scalar_tensor_tensor(out=a["ie"][:, 0, :], in0=a["ie"][:, 0, :], scalar=float(E_KEYS),
                                                in1=a["ie"][:, 1, :], op0=ALU.mult, op1=ALU.add))
                    signal(v.tensor_scalar(a["idx"][:, i, :], a["ie"][:, 0, :], float(l * NEXP), None, ALU.add),
                           "pk_idx", at, n)

            for r, (kind, l) in enumerate(RUNS):
                at = At(r)
                nq = q_tiles(l)
                nq_tok = nq * P
                units = RUN_UNITS[r]
                meet_before(dve, r)
                if kind == "mod":
                    m = arena_mod()
                    dve.wait_ge(S["mod_sig"], at("mod_sig", 1))
                    v.tensor_copy(par_col[:, :], bank[4][:, 0:48])
                    v.tensor_tensor(c_col[:, :, :], bank[4][:, 32:48].rearrange("p (s k) -> p s k", s=2),
                                    m["sig"].rearrange("p (s k) -> p s k", s=2), ALU.mult)\
                        .then_inc(S["mod_act_in"], 1)
                    dve.wait_ge(S["stage_in"], 16 * 14 * (l + 1))
                    for j, n in enumerate(units):
                        b = wait_group(n, 0)
                        v.tensor_tensor(m["rows"][:, 512 * j:512 * (j + 1)], b[0:2, :],
                                        m["b_mod"][:, 512 * j:512 * (j + 1)], ALU.add)\
                            .then_inc(S["evac_dve"], 1)
                    dve.wait_ge(S["evac_dve"], evac_count(units[-1], 0))
                    v.tensor_copy(gate_rows[:, 0, :], m["rows"][:, 2 * D:3 * D])
                    v.tensor_copy(gate_rows[:, 1, :], m["rows"][:, 5 * D:6 * D]).then_inc(S["mod_rows"], 1)
                    dve.wait_ge(S["mod_colT"], at("mod_colT", 1))
                    link(v.tensor_copy(mod_col[:, :, :, :],
                                       bank[5][:, 0:64].rearrange("p (i k s) -> p i k s", i=4, k=KC)))
                    for w in range(2):
                        v.scalar_tensor_tensor(out=scale_col[:, w, :, :], in0=mod_col[:, 1 + 2 * w, :, :], scalar=1.0,
                                               in1=par_col[:, 8 * w:8 * w + 8].unsqueeze(2).broadcast_to([P, KC, 2]),
                                               op0=ALU.add, op1=ALU.mult)
                elif kind in ("norm1", "norm2"):
                    a = arena_norm()
                    w = 0 if kind == "norm1" else 1
                    n = NT if kind == "norm1" else nq
                    dve.wait_ge(S["norm_sq"], at("norm_sq", 1))
                    v.tensor_scalar(small[:, 4:4 + n], small[:, 0:n], 1.0 / D, EPS, ALU.mult, ALU.add)\
                        .then_inc(S["norm_var"], 1)
                    dve.wait_ge(S["norm_std"], at("norm_std", 1))
                    link(v.reciprocal(small[:, 12:12 + n], small[:, 8:8 + n]))

                    def normalise(i):
                        if i >= 2:
                            dve.wait_ge(S["norm_T"], at("norm_T", 2 * i - 2))
                        v.tensor_scalar(a["xn"][:, i % 2, :], x_sb[:, i, :], small[:, 12 + i:13 + i], None, ALU.mult)\
                            .then_inc(S["norm_x"], 1)

                    normalise(0)
                    for i in range(n):
                        s = 0 if i < LT else 1
                        if i + 1 < n:
                            normalise(i + 1)
                        for half in range(2):
                            j = 2 * i + half
                            dve.wait_ge(S["norm_T"], at("norm_T", j + 1))
                            for c in range(4):
                                k = 4 * half + c
                                last = v.tensor_scalar(hT[:, k, P * i:P * (i + 1)],
                                                       bank[4 + j % 4][:, P * c:P * (c + 1)],
                                                       scale_col[:, w, k, s:s + 1], mod_col[:, 2 * w, k, s:s + 1],
                                                       ALU.mult, ALU.add)
                            last.then_inc(S["norm_h"], 1)
                elif kind in ("attnA", "attnB"):
                    br = 0 if kind == "attnA" else 1
                    a = arena_attn(br)
                    kw = 128 if br == 0 else 512
                    for i in range(NT):
                        w = kw + (512 if i < nq else 0)
                        nh = w // HD
                        if i < nq:
                            dve.wait_ge(S["evac_act"], evac_count(units[1], i))
                        else:
                            dve.wait_ge(S["evac_act"], evac_count(units[0], i))
                        link(v.tensor_tensor(a["tmp"][:, 0:w], a["qk"][:, i, 0:w], a["qk"][:, i, 0:w], ALU.mult))
                        link(v.tensor_reduce(a["ss"][:, i, 0:nh], a["tmp"][:, 0:w].rearrange("p (h d) -> p h d", d=HD),
                                             AX.X, ALU.add))
                        v.tensor_scalar(a["ss"][:, i, 0:nh], a["ss"][:, i, 0:nh], 1.0 / HD, EPS, ALU.mult, ALU.add)\
                            .then_inc(S["prep_var"], 1)
                    dve.wait_ge(S["arena_in"], 16 * arena_in_count(r))
                    if br == 1:
                        for j in range(4 * LT):
                            dve.wait_ge(S["bias_turned"], at("bias_turned", j + 1))
                            v.tensor_tensor(a["bias"][:, j // 4, 2 * (j % 4):2 * (j % 4) + 2, :],
                                            bank[4 + j % 4][:, :].rearrange("p (h k) -> p h k", h=2),
                                            a["mask"][:, j // 4, :].unsqueeze(1).broadcast_to([P, 2, SEQ]), ALU.add)\
                                .then_inc(S["bias_ready"], 1)
                    for i in range(NT):
                        w = kw + (512 if i < nq else 0)
                        nh = w // HD
                        dve.wait_ge(S["prep_std"], at("prep_std", i + 1))
                        link(v.reciprocal(a["ss"][:, i, 0:nh], a["ss"][:, i, 0:nh]))
                        qk = a["qk"][:, i, 0:w].rearrange("p (h d) -> p h d", d=HD)
                        link(v.tensor_tensor(qk, qk, a["ss"][:, i, 0:nh].unsqueeze(2).broadcast_to([P, nh, HD]), ALU.mult))
                        for part, (h0, h1) in enumerate(((0, kw // HD), (kw // HD, nh))):
                            if h1 == h0:
                                continue
                            last = v.tensor_tensor(qk[:, h0:h1, :], qk[:, h0:h1, :],
                                                   head_w[:, 2 * br + part, :].unsqueeze(1).broadcast_to([P, h1 - h0, HD]),
                                                   ALU.mult)
                            if br == 0 and i < LT:
                                link(last)
                            elif h1 == nh:
                                last.then_inc(S["prep_qk"], 1)
                        if br == 0 and i < LT:
                            q5 = a["qk"][:, i, 0:w].rearrange("p (h c s d) -> p h c s d", c=2, s=2, d=16)
                            t5 = a["tmp"][:, 0:w].rearrange("p (h c s d) -> p h c s d", c=2, s=2, d=16)
                            sn = sin[:, i, :].rearrange("p (c s d) -> p c s d", c=2, s=2)
                            for s in range(2):
                                last = v.tensor_tensor(t5[:, :, :, s, :], q5[:, :, :, 1 - s, :],
                                                       sn[:, :, s, :].unsqueeze(1).broadcast_to([P, nh, 2, 16]), ALU.mult)
                            link(last)
                            link(v.tensor_tensor(qk, qk, cos[:, i, :].unsqueeze(1).broadcast_to([P, nh, HD]), ALU.mult))
                            v.tensor_tensor(a["qk"][:, i, 0:w], a["qk"][:, i, 0:w], a["tmp"][:, 0:w], ALU.add)\
                                .then_inc(S["prep_qk"], 1)
                    if br == 1:
                        dve.wait_ge(S["bias_ready"], at("bias_ready", 4 * LT))

                    def heads_norm(i):
                        dve.wait_ge(S["heads_out"], at("heads_out", i + 1))
                        if i >= 2:
                            dve.wait_ge(S["heads_T"], at("heads_T", i - 1))
                        link(v.reciprocal(a["rinv"][:, 8 * i:8 * i + 8], a["rsum"][:, 8 * i:8 * i + 8]))
                        v.tensor_tensor(a["o"][:, i % 2, :].rearrange("p (h d) -> p h d", h=8),
                                        bank[2 + i % 2][:, :].rearrange("p (h d) -> p h d", h=8),
                                        a["rinv"][:, 8 * i:8 * i + 8].unsqueeze(2).broadcast_to([P, 8, HD]), ALU.mult)\
                            .then_inc(S["heads_normed"], 1)

                    for u, (i, h) in enumerate(ATT_UNITS[l]):
                        dve.wait_ge(S["scores"], at("scores", u + 1))
                        if u >= 2:
                            dve.wait_ge(S["probs_T"], at("probs_T", u - 1))
                        b = bank[4 + u % 2]
                        sc = a["S"][:, u % 2, :]
                        lo, hi = 0 if i < LT else SEQ, 513 if br == 0 else 512
                        if i < LT:
                            v.scalar_tensor_tensor(out=sc[:, 0:SEQ], in0=b[:, 0:SEQ], scalar=HD ** -0.5,
                                                   in1=a["mask"][:, i, :] if br == 0 else a["bias"][:, i, h, :],
                                                   op0=ALU.mult, op1=ALU.add)
                        if br == 0:
                            v.tensor_copy(sc[:, 512:513], sink[:, h:h + 1])
                        link(v.tensor_scalar(sc[:, SEQ:512], b[:, SEQ:512], HD ** -0.5, None, ALU.mult))
                        c = 8 * i + h
                        v.tensor_reduce(a["nmax"][:, c:c + 1], sc[:, lo:hi], AX.X, ALU.max, negate=True)\
                            .then_inc(S["score_max"], 1)
                        if h == 1 and i >= 1:
                            heads_norm(i - 1)
                    heads_norm(nq - 1)
                elif kind in ("gla0", "gla1"):
                    hp = int(kind[-1])
                    g = arena_gla()
                    ua, uk, uq, uv, ur = units
                    Pv = [z.rearrange("p (t h i) -> p t h i", t=NT, h=2) for z in g["P"]]
                    for d in range(2):
                        last = v.memset(Pv[d][:, :, :, 0:1], 0.0)
                    link(last)
                    for j in range(4):
                        d, hh = divmod(j, 2)
                        c = 16 + 4 * d + 2 * hp + hh
                        dve.wait_ge(S["gla_soft"], at("gla_soft", j + 1))
                        signal(v.tensor_scalar(g["t4"][j], bank[4 + j][:, :], par_col[:, c:c + 1], 0.0, ALU.add, ALU.min),
                               "gla_zfree", at, j + 1)
                        link(v.tensor_tensor(Pv[d][:, :, hh, 1:PADW], g["t4"][j].rearrange("p (t i) -> p t i", t=NT),
                                             g["t1"][j].rearrange("p (t i) -> p t i", t=NT), ALU.subtract))
                    dve.wait_ge(S["arena_in"], 16 * arena_in_count(r))
                    for d in range(2):
                        last = v.tensor_tensor_scan(g["P"][d], g["reset"], g["P"][d], 0.0, ALU.mult, ALU.add)
                    signal(last, "gla_ready", at, 1)

                    def end(d, n):
                        return Pv[d][:, 0:n, :, P:P + 1].broadcast_to([P, n, 2, P])
                    v.tensor_tensor(g["KF"][0][:, :, :, :], end(0, NT), Pv[0][:, :, :, 1:PADW], ALU.subtract)\
                        .then_inc(S["gla_diff"], 1)
                    v.tensor_tensor(g["QF"][1][:, 0:nq, :, :], end(1, nq), Pv[1][:, 0:nq, :, 0:P], ALU.subtract)\
                        .then_inc(S["gla_diff"], 1)

                    def diff(lv):
                        hf = 1 << lv
                        eq, ek = g["E"][lv % 2]
                        for i in range(nq):
                            def halves(z):
                                return z.rearrange("p h (b s e) -> p h b s e", s=2, e=hf)
                            nb = P // (2 * hf)
                            inc = [halves(Pv[d][:, i, :, 1:PADW]) for d in range(2)]
                            exc = [halves(Pv[d][:, i, :, 0:P]) for d in range(2)]
                            mid = [exc[d][:, :, :, 1, 0:1].broadcast_to([P, 2, nb, hf]) for d in range(2)]
                            q5, k5 = halves(eq[:, i, :, :]), halves(ek[:, i, :, :])
                            v.tensor_tensor(q5[:, :, :, 1, :], inc[0][:, :, :, 1, :], mid[0], ALU.subtract)
                            v.tensor_tensor(k5[:, :, :, 0, :], mid[0], inc[0][:, :, :, 0, :], ALU.subtract)
                            v.tensor_tensor(q5[:, :, :, 0, :], mid[1], exc[1][:, :, :, 0, :], ALU.subtract)
                            last = v.tensor_tensor(k5[:, :, :, 1, :], exc[1][:, :, :, 1, :], mid[1], ALU.subtract)
                        last.then_inc(S["gla_diff"], 1)

                    diff(0)
                    dve.wait_ge(S["evac_act"], evac_count(uq, 1))
                    for n, (z, e, w, cnt) in enumerate(((g["KF"][1], 1, g["k"], NT), (g["KF"][0], 3, g["k"], NT),
                                                        (g["QF"][0], 2, g["q"], nq), (g["QF"][1], 4, g["q"], nq))):
                        dve.wait_ge(S["gla_exp"], at("gla_exp", e))
                        v.tensor_tensor(z[:, 0:cnt, :, :], z[:, 0:cnt, :, :], w[:, 0:cnt, :, :], ALU.mult)\
                            .then_inc(S["gla_fac"], 1)
                    steps = [(d, s) for s in range(3) for d in range(2)]
                    for n, (d, s) in enumerate(steps):
                        i = CHAIN[d][s]
                        dve.wait_ge(S["gla_upd"], at("gla_upd", n + 1))
                        b = bank[6 + n % 2]
                        if s == 0:
                            last = v.tensor_copy(g["S"][d][:, 0, :, :], b[:, :].rearrange("p (h v) -> p h v", h=2))
                        else:
                            dve.wait_ge(S["gla_state"], at("gla_state", n - 1))
                            for hh in range(2):
                                last = v.scalar_tensor_tensor(out=g["S"][d][:, s, hh, :], in0=g["S"][d][:, s - 1, hh, :],
                                                              scalar=g["dec"][:, d, i, hh:hh + 1],
                                                              in1=b[:, CDV * hh:CDV * (hh + 1)],
                                                              op0=ALU.mult, op1=ALU.add)
                        last.then_inc(S["gla_state"], 1)

                    per = 4

                    def keep(m):
                        dve.wait_ge(S["gla_att"], at("gla_att", m + 1))
                        for h in range(nq * 2 // per):
                            b = bank[4 + 2 * (m % 2) + h][:, :].rearrange("p (m i) -> p m i", i=P)
                            dst = g["att"][:, per * h:per * (h + 1), :]
                            if m == 0:
                                last = v.tensor_tensor(dst, b, g["diag2"].unsqueeze(1).broadcast_to([P, per, P]), ALU.mult)
                            else:
                                last = v.copy_predicated(dst, g["lvl"][:, m - 1, :].unsqueeze(1).broadcast_to([P, per, P]), b)
                        signal(last, "gla_attfree", at, m + 1)

                    for lv in range(LEVELS):
                        if lv + 1 < LEVELS:
                            if lv == 0:
                                dve.wait_ge(S["gla_kT"], at("gla_kT", 6))
                            else:
                                dve.wait_ge(S["gla_att"], at("gla_att", lv + 1))
                            diff(lv + 1)
                        dve.wait_ge(S["gla_exp"], at("gla_exp", 5 + lv))
                        eq, ek = g["E"][lv % 2]
                        v.tensor_tensor(eq[:, 0:nq, :, :], eq[:, 0:nq, :, :], g["q"][:, 0:nq, :, :], ALU.mult)
                        v.tensor_tensor(ek[:, 0:nq, :, :], ek[:, 0:nq, :, :], g["k"][:, 0:nq, :, :], ALU.mult)\
                            .then_inc(S["gla_fac"], 1)
                        keep(lv)
                    keep(LEVELS)
                    for i in range(nq):
                        dve.wait_ge(S["gla_osq"], at("gla_osq", i + 1))
                        v.tensor_scalar(g["ss"][:, 8 + 2 * i:10 + 2 * i], g["ss"][:, 2 * i:2 * i + 2], 1.0 / CDV, EPS,
                                        ALU.mult, ALU.add).then_inc(S["gla_ovar"], 1)
                    for i in range(nq):
                        dve.wait_ge(S["gla_ostd"], at("gla_ostd", i + 1))
                        link(v.reciprocal(g["ss"][:, 2 * i:2 * i + 2], g["ss"][:, 8 + 2 * i:10 + 2 * i]))
                        if i >= 2:
                            dve.wait_ge(S["gla_oT"], at("gla_oT", i - 1))
                        y = g["y"][:, i % 2, :]
                        for hh in range(2):
                            last = v.scalar_tensor_tensor(out=y[:, CDV * hh:CDV * (hh + 1)],
                                                          in0=bank[4 + i][:, CDV * hh:CDV * (hh + 1)],
                                                          scalar=g["ss"][:, 2 * i + hh:2 * i + hh + 1], in1=gn[:, :],
                                                          op0=ALU.mult, op1=ALU.mult)
                        link(last)
                        link(v.tensor_tensor(y, y, g["r"][:, i, :], ALU.mult))
                        dve.wait_ge(S["gla_sg"], at("gla_sg", i + 1))
                        v.tensor_tensor(y, y, g["sg"][:, i % 2, :], ALU.mult).then_inc(S["gla_oy"], 1)
                elif kind == "merge":
                    a = arena_merge()
                    gates = [n for n in units if UNITS[n]["engine"] == "mix"]
                    m = 0
                    for q, n in enumerate(gates):
                        for c in range(2):
                            dc = 2 * (q % 4) + c
                            b = wait_group(n, 2 * c + 1)
                            dve.wait_ge(S["evac_act"], evac_count(n, 2 * c))
                            y, sg, tmp = a["y"][:, dc, 0:nq_tok], a["sig"][:, m % 2, 0:nq_tok], a["tmp"][:, m % 2, 0:nq_tok]
                            if q < 4:
                                v.tensor_tensor(y, b[:, 0:nq_tok], sg, ALU.mult).then_inc(S["evac_dve"], 1)
                            else:
                                link(v.tensor_tensor(tmp, b[:, 0:nq_tok], sg, ALU.mult))
                                v.tensor_tensor(y, y, tmp, ALU.add).then_inc(S["evac_dve"], 1)
                            m += 1
                    for s in range(4):
                        dve.wait_ge(S["gate_b"], at("gate_b", s + 1))
                        last = v.tensor_copy(a["gb"][:, s // 2, 512 * (s % 2):512 * (s % 2) + 512], bank[4 + s][:, :])
                        last.then_inc(S["gate_copied"], 1)
                    dve.wait_ge(S["gate_copied"], at("gate_copied", 4))
                    for half, n in enumerate(units[-2:]):
                        cols = slice(512 * half, 512 * (half + 1))
                        for i in range(nq):
                            b = wait_group(n, i)
                            tmp = a["tmp"][:, i % 2, :]
                            link(v.tensor_tensor(tmp, b[:, :], a["gb"][:, 0 if i < LT else 1, cols], ALU.mult))
                            v.tensor_tensor(x_sb[:, i, cols], x_sb[:, i, cols], tmp, ALU.add).then_inc(S["evac_dve"], 1)
                elif kind == "pick":
                    a = arena_peer()
                    for j in range(4):
                        b = wait_group(units[0], j)
                        v.tensor_scalar(a["skT"][:, 4 * j:4 * j + 4, :], b[:, :].rearrange("p (g n) -> p g n", g=4),
                                        par_col[:, 24:25], None, ALU.mult).then_inc(S["evac_dve"], 1)
                    for gr in range(16):
                        dve.wait_ge(S["pk_score"], at("pk_score", gr + 1))
                        signal(v.tensor_copy(a["s"][:, 0:nq, gr, :],
                                             bank[4 + gr % 3][:, 0:nq_tok].rearrange("p (t n) -> p t n", t=nq)),
                               "pk_scopied", at, gr + 1)
                        if gr in (5, 11):
                            choose(0, gr // 6, l, at, 1)
                    v.tensor_scalar(a["rstd"].rearrange("p (g t) -> p g t", t=NT)[:, :, 0:nq],
                                    bank[7][:, 0:16 * nq].rearrange("p (g t) -> p g t", t=nq), 1.0 / P, EPS,
                                    ALU.mult, ALU.add).then_inc(S["pk_var"], 1)
                    dve.wait_ge(S["pk_std"], at("pk_std", 1))
                    rstd = a["rstd"].rearrange("p (g t) -> p g t", t=NT)[:, :, 0:nq]
                    link(v.reciprocal(rstd, rstd))
                    for part in range(2, 8):
                        choose(0, part, l, at, 1)
                elif kind == "expert":
                    e = arena_peer()
                    if l == 0:
                        for n in range(GB):
                            v.memset(e["acc"][:, P * n:P * (n + 1)], 0.0).then_inc(S["ex_used"], 1)
                    for s in range(4):
                        dve.wait_ge(S["gate_b"], at("gate_b", s + 1))
                        v.tensor_copy(e["gb"][:, s // 2, 512 * (s % 2):512 * (s % 2) + 512], bank[4 + s][:, :])\
                            .then_inc(S["gate_copied"], 1)
                    used0 = BASES[r].get("ex_used", 0)
                    rows0 = used0 // GB
                    for i in range(nq):
                        for table in range(2):
                            ps = 2 * i + table
                            if table == 1:
                                g3 = e["gval"][:, i, :].rearrange("p (h k) -> p h k", h=E_HEADS)
                                if i >= 1:
                                    dve.wait_ge(S["pk_exp"], at("pk_exp", i))
                                link(v.tensor_reduce(e["gs"], g3, AX.X, ALU.add))
                                link(v.reciprocal(e["gs"], e["gs"]))
                                link(v.tensor_tensor(g3, g3, e["gs"].unsqueeze(2).broadcast_to([P, E_HEADS, TOPK]),
                                                     ALU.mult))
                                dve.wait_ge(S["ex_gelu"], at("ex_gelu", i + 1))
                                v.tensor_tensor(e["coef"], e["gel"], e["gval"][:, i, :], ALU.mult)
                                signal(v.memset(e["acc"], 0.0), "ex_coef", at, i + 1)
                            for part, (it0, it1) in enumerate(((0, 1), (1, 3), (3, 5), (5, 7), (7, 8))):
                                with dve.Fori(it0, it1) as it:
                                    for n in range(16):
                                        s = n % GB
                                        dve.wait_ge(S["ex_used"], it * 16 + (used0 + GB + ps * PK + n))
                                        if table == 0:
                                            dve.wait_ge(row_in[s], it * 32 + 16 * (rows0 + ps * (PK // GB) + n // GB + 1))
                                            v.scalar_tensor_tensor(
                                                out=e["junk"][:, n % 2, :], in0=e["rows"][:, s, :], scalar=1.0,
                                                in1=e["tok"][:, i, :], op0=ALU.mult, op1=ALU.mult,
                                                accum_out=e["dots"][:, bass.ds(it * 16 + n, 1)]).then_inc(S["ex_used"], 1)
                                        else:
                                            dve.wait_ge(S["ex_sums"], it * 16 + at("ex_sums", DB + i * PK + n + 1))
                                            v.scalar_tensor_tensor(
                                                out=e["acc"][:, HALF:D], in0=e["rows"][:, s, HALF:D],
                                                scalar=e["coef"][:, bass.ds(it * 16 + n, 1)],
                                                in1=e["acc"][:, HALF:D], op0=ALU.mult, op1=ALU.add).then_inc(S["ex_used"], 1)
                                if part < 4 and i + 1 < nq:
                                    choose(i + 1, 4 * table + part, l, at, i + 1)
                        dve.wait_ge(S["ex_used"], used0 + GB + (2 * i + 2) * PK)
                        dve.wait_ge(S["ex_total"], at("ex_total", i + 1))
                        gate = e["gb"][:, 0 if i < LT else 1, :]
                        v.tensor_tensor(e["acc"][:, 0:HALF], bank[i % 2][:, :], gate[:, 0:HALF], ALU.mult)
                        link(v.tensor_tensor(e["acc"][:, HALF:D], e["acc"][:, HALF:D], gate[:, HALF:D], ALU.mult))
                        link(v.tensor_tensor(x_sb[:, i, :], x_sb[:, i, :], e["acc"], ALU.add))
                dve.drain().then_inc(S["phase_end"], 1)


def shape_constants():
    pos = np.arange(SEQ)
    row, col = (pos // GRID_W).astype(np.float32)[:, None], (pos % GRID_W).astype(np.float32)[:, None]
    nf = HD // 4
    inv = (np.float32(10000.0) ** (-np.arange(nf, dtype=np.float32) / np.float32(nf))).astype(np.float32)
    ang = np.concatenate([row * inv, row * inv, col * inv, col * inv], axis=-1).astype(np.float32)
    sign = np.repeat(np.array([-1, 1, -1, 1], np.float32), nf)

    def tiles(a):
        return np.ascontiguousarray(a.reshape(LT, P, -1).transpose(1, 0, 2)).astype(np.float32)
    dist = np.abs(pos[:, None] - pos[None, :])
    mask_a = np.where(dist <= 128, 0.0, NEG)
    c = pos % GRID_W
    start = np.clip(c - NA_COLS // 2, 0, GRID_W - NA_COLS)
    mask_b = np.where((c[None, :] >= start[:, None]) & (c[None, :] < start[:, None] + NA_COLS), 0.0, NEG)
    i = np.arange(P)
    lvl = np.zeros((P, LEVELS, P), np.int32)
    for lv in range(LEVELS):
        same = (i[:, None] >> (lv + 1)) == (i[None, :] >> (lv + 1))
        lvl[:, lv, :] = same & ((i[:, None] >> lv) != (i[None, :] >> lv))
    reset = np.ones((P, NT * 2, PADW), np.float32)
    reset[:, :, 0] = 0.0
    pick_row = np.zeros((2, 2, P), np.float32)
    pick_row[0, 0] = pick_row[1, 1] = 1.0
    turn = np.kron(np.eye(2), np.eye(GRID_W)[::-1]).astype(np.float32)
    return dict(ident=np.eye(P, dtype=np.float32), turn=turn, cos=tiles(np.cos(ang)), sin=tiles(np.sin(ang) * sign),
                mask_a=tiles(mask_a), mask_b=tiles(mask_b), lvl=lvl, diag2=2.0 * np.eye(P, dtype=np.float32),
                reset=reset.reshape(P, -1), pick_row=pick_row,
                iota=np.tile(np.arange(TOPK, dtype=np.float32), (P, 1)))


_INS = ["x", "c", "ctx", "c_ctx", "w_mod", "b_mod", "norm1", "norm2", "w_in", "qn_a", "kn_a", "sink_a", "qn_b",
        "kn_b", "rpb_b", "wa2_f", "ba_f", "wa2_b", "ba_b", "gn_c", "w_oa", "w_ob", "w_oc", "w_out", "w_pq", "pq_g",
        "sub_keys", "peer_u", "peer_v"]


def kernel(**inputs):
    import concourse.bacc as bacc
    from concourse.bass_utils import run_bass_kernel_spmd

    nc = bacc.Bacc("TRN2", target_bir_lowering=False, num_devices=1)
    arrays, aps = {}, {}
    for name, value in [(n, inputs[n]) for n in _INS] + list(shape_constants().items()):
        a = np.ascontiguousarray(value)
        arrays[f"in_{name}"] = a
        aps[name] = nc.dram_tensor(f"in_{name}", a.shape, mybir.dt.from_np(a.dtype), kind="ExternalInput").ap()
    out = nc.dram_tensor("out", (1, SEQ, D), FP, kind="ExternalOutput").ap()
    backbone(nc, aps, out)
    return run_bass_kernel_spmd(nc, [arrays], core_ids=[0]).results[0]["out"]
```
